# Optimizing a Trainium2 kernel written in Bass

```python
import math
import jax
import jax.numpy as jnp
from jax import lax
import numpy as np

D_MODEL = 1024
BATCH = 1
SEQ = 256
DEPTH = 2
DEC_BATCH = 1
DEC_SEQ = 64
PAST_LEN = 128

CHUNK = 64
H_A = 4
DK_A = 128
DV_A = 128
CONV_W = 4
H_B = 4
DH_B = 64
BAND_CHUNKS = 8
REL_CLIP = 128
H_C = 4
DK_C = 64
DV_C = 64
ROPE_BASE = 10000.0
D_FF = 2816
EPS = 1e-6
NEG_INF = -1e30

MIX_A = H_A * DV_A
MIX_B = H_B * DH_B
MIX_C = H_C * DV_C
MIX = MIX_A + MIX_B + MIX_C
CONV_DIM = 2 * H_A * DK_A + H_A * DV_A
BAND = BAND_CHUNKS * CHUNK
IN_SIZES = (CONV_DIM, MIX_A, H_A, H_A, MIX_B, MIX_B, MIX_B, H_C * DK_C, H_C * DK_C, MIX_C, MIX_C)
IN_COLS = sum(IN_SIZES)

kernel_name = "hybrid_streaming_encoder_step"

def rmsnorm(x, g):
    xf = x.astype(jnp.float32)
    y = xf * lax.rsqrt(jnp.mean(xf * xf, axis=-1, keepdims=True) + EPS)
    return (y * g.astype(jnp.float32)).astype(x.dtype)

def head_layernorm(x):
    xc = x - jnp.mean(x, axis=-1, keepdims=True)
    return xc * lax.rsqrt(jnp.mean(xc * xc, axis=-1, keepdims=True) + EPS)

def l2norm(x):
    return x * lax.rsqrt(jnp.sum(x * x, axis=-1, keepdims=True) + EPS)

def swiglu(x, w_gate, w_up, w_down):
    return (jax.nn.silu(x @ w_gate) * (x @ w_up)) @ w_down

def split_cols(u, sizes):
    out, o = [], 0
    for s in sizes:
        out.append(u[..., o:o + s])
        o += s
    return out

def rope(x, pos):
    half = x.shape[-1] // 2
    inv_freq = jnp.exp(-math.log(ROPE_BASE) * jnp.arange(half, dtype=jnp.float32) / half)
    ang = pos.astype(jnp.float32)[:, None] * inv_freq[None, :]
    cos, sin = jnp.cos(ang)[:, None, :], jnp.sin(ang)[:, None, :]
    x1, x2 = x[..., :half], x[..., half:]
    return jnp.concatenate([x1 * cos - x2 * sin, x1 * sin + x2 * cos], axis=-1)

def causal_conv(u, buf, w):
    L = u.shape[1]
    up = jnp.concatenate([buf.astype(u.dtype), u], axis=1)
    y = up[:, 0:L] * w[0]
    for j in range(1, CONV_W):
        y = y + up[:, j:j + L] * w[j]
    return jax.nn.silu(y), up[:, -(CONV_W - 1):]

def chunk_scan(step, state, xs):
    L = xs[0].shape[2]
    cl = min(CHUNK, L)
    nc = L // cl

    def to_chunks(a):
        a = a.reshape(a.shape[:2] + (nc, cl) + a.shape[3:])
        return jnp.moveaxis(a, 2, 0)

    state, out = lax.scan(lambda s, c: step(s, *c), state, tuple(to_chunks(a) for a in xs))
    out = jnp.moveaxis(out, 0, 2)
    return state, out.reshape(out.shape[:2] + (L,) + out.shape[4:])

def gdn_chunk(S, q, k, v, g, beta):
    L = q.shape[2]
    decay = jnp.cumsum(g, axis=-1)
    tril = jnp.tril(jnp.ones((L, L), bool))
    strict = jnp.tril(jnp.ones((L, L), bool), -1)
    diff = decay[..., :, None] - decay[..., None, :]
    lmask = jnp.where(tril, jnp.exp(jnp.where(tril, diff, 0.0)), 0.0)
    kb = k * beta[..., None]
    a_low = jnp.where(strict, jnp.einsum('bhik,bhjk->bhij', kb, k) * lmask, 0.0)
    m = a_low + jnp.eye(L, dtype=jnp.float32)
    rhs = jnp.concatenate([v * beta[..., None], kb * jnp.exp(decay)[..., None]], axis=-1)
    sol = lax.linalg.triangular_solve(m, rhs, left_side=True, lower=True, unit_diagonal=True)
    val, kcd = sol[..., :DV_A], sol[..., DV_A:]
    v_new = val - jnp.einsum('bhlk,bhkv->bhlv', kcd, S)
    attn = jnp.einsum('bhik,bhjk->bhij', q, k) * lmask
    o = (jnp.einsum('bhlk,bhkv->bhlv', q * jnp.exp(decay)[..., None], S)
         + jnp.einsum('bhij,bhjv->bhiv', attn, v_new))
    dl = decay[..., -1:]
    S_new = (S * jnp.exp(dl)[..., None]
             + jnp.einsum('bhlk,bhlv->bhkv', k * jnp.exp(dl - decay)[..., None], v_new))
    return S_new, o

def retention_log_decay():
    return jnp.log1p(-jnp.exp2(-5.0 - jnp.arange(H_C, dtype=jnp.float32)))

def ret_chunk(R, q, k, v, lg):
    L = q.shape[2]
    n = jnp.arange(L, dtype=jnp.float32)
    diff = n[:, None] - n[None, :]
    causal = diff >= 0
    dmask = jnp.where(causal, jnp.exp(lg[:, None, None] * jnp.where(causal, diff, 0.0)), 0.0)
    inner = jnp.einsum('bhij,bhjv->bhiv', jnp.einsum('bhik,bhjk->bhij', q, k) * dmask, v)
    cross = jnp.einsum('bhlk,bhkv->bhlv', q * jnp.exp(lg[:, None] * (n + 1.0))[..., None], R)
    R_new = (R * jnp.exp(lg * L)[:, None, None]
             + jnp.einsum('bhlk,bhlv->bhkv', k * jnp.exp(lg[:, None] * (L - 1.0 - n))[..., None], v))
    return R_new, inner + cross

def band_attn_prompt(q, k, v, rel_bias):
    B_, T = q.shape[:2]
    nc = T // CHUNK
    f32 = jnp.float32

    def chunks(a):
        return a.astype(f32).reshape(B_, nc, CHUNK, H_B, DH_B)

    def band(a):
        ap = jnp.pad(chunks(a), ((0, 0), (BAND_CHUNKS, 0), (0, 0), (0, 0), (0, 0)))
        return jnp.concatenate([ap[:, o:o + nc] for o in range(BAND_CHUNKS + 1)], axis=2)

    kband, vband = band(k), band(v)
    s = jnp.einsum('bnqhd,bnkhd->bnhqk', chunks(q), kband) * DH_B ** -0.5
    j = jnp.arange((BAND_CHUNKS + 1) * CHUNK)
    i = jnp.arange(CHUNK)
    rel = j[None, :] - BAND - i[:, None]
    s = s + rel_bias.astype(f32)[:, jnp.clip(rel, -REL_CLIP, REL_CLIP) + REL_CLIP]
    valid = (jnp.arange(nc)[:, None] - BAND_CHUNKS + j[None, :] // CHUNK) >= 0
    s = jnp.where(valid[None, :, None, None, :], s, NEG_INF)
    p = jax.nn.softmax(s, axis=-1)
    o = jnp.einsum('bnhqk,bnkhd->bnqhd', p, vband)
    return o.reshape(B_, T, MIX_B)

def band_attn_sample(q, k, v, ck, cv, rel_bias):
    B_, L = q.shape[:2]
    P = ck.shape[1]
    f32 = jnp.float32
    kk = jnp.concatenate([ck.astype(f32), k.astype(f32)], axis=1)
    vv = jnp.concatenate([cv.astype(f32), v.astype(f32)], axis=1)
    s = jnp.einsum('bqhd,bkhd->bhqk', q.astype(f32), kk) * DH_B ** -0.5
    rel = (jnp.arange(P + L) - P)[None, :] - jnp.arange(L)[:, None]
    s = s + rel_bias.astype(f32)[:, jnp.clip(rel, -REL_CLIP, REL_CLIP) + REL_CLIP]
    p = jax.nn.softmax(s, axis=-1)
    o = jnp.einsum('bhqk,bkhd->bqhd', p, vv)
    return o.reshape(B_, L, MIX_B)

def token_mix(h, w_in, conv_w, a_log, dt_bias, gdn_norm, rel_bias, w_out,
              conv_buf, s_gdn, s_ret, band_k, band_v, pos0):
    B_, L, _ = h.shape
    f32 = jnp.float32
    (u_qkv, z_a, b_a, a_a, q_b, k_b, v_b, q_c, k_c, v_c, g_c) = split_cols(h @ w_in, IN_SIZES)
    hs = lambda a: jnp.swapaxes(a, 1, 2)

    u_conv, conv_new = causal_conv(u_qkv, conv_buf, conv_w)
    qa, ka, va = split_cols(u_conv.astype(f32), (H_A * DK_A, H_A * DK_A, H_A * DV_A))
    qa = l2norm(qa.reshape(B_, L, H_A, DK_A)) * DK_A ** -0.5
    ka = l2norm(ka.reshape(B_, L, H_A, DK_A))
    va = va.reshape(B_, L, H_A, DV_A)
    g = -jnp.exp(a_log.astype(f32)) * jax.nn.softplus(a_a.astype(f32) + dt_bias.astype(f32))
    beta = jax.nn.sigmoid(b_a.astype(f32))
    s_gdn_new, oa = chunk_scan(gdn_chunk, s_gdn.astype(f32), (hs(qa), hs(ka), hs(va), hs(g), hs(beta)))
    oa = rmsnorm(hs(oa), gdn_norm) * jax.nn.silu(z_a.astype(f32).reshape(B_, L, H_A, DV_A))

    qb = q_b.reshape(B_, L, H_B, DH_B)
    kb = k_b.reshape(B_, L, H_B, DH_B)
    vb = v_b.reshape(B_, L, H_B, DH_B)
    if band_k is None:
        ob = band_attn_prompt(qb, kb, vb, rel_bias)
        keep = min(BAND, L)
        kb_new, vb_new = kb[:, -keep:], vb[:, -keep:]
    else:
        ob = band_attn_sample(qb, kb, vb, band_k.astype(kb.dtype), band_v.astype(vb.dtype), rel_bias)
        kb_new, vb_new = kb, vb

    pos = pos0 + jnp.arange(L)
    qc = rope(q_c.astype(f32).reshape(B_, L, H_C, DK_C), pos)
    kc = rope(k_c.astype(f32).reshape(B_, L, H_C, DK_C), pos) * DK_C ** -0.5
    vc = v_c.astype(f32).reshape(B_, L, H_C, DV_C)
    lg = retention_log_decay()
    s_ret_new, oc = chunk_scan(lambda s, q, k, v: ret_chunk(s, q, k, v, lg), s_ret.astype(f32),
                               (hs(qc), hs(kc), hs(vc)))
    oc = head_layernorm(hs(oc)) * jax.nn.silu(g_c.astype(f32).reshape(B_, L, H_C, DV_C))

    o = jnp.concatenate([oa.reshape(B_, L, MIX_A), ob.reshape(B_, L, MIX_B), oc.reshape(B_, L, MIX_C)], axis=-1)
    out = o.astype(h.dtype) @ w_out
    return out, (s_gdn_new, conv_new, kb_new, vb_new, s_ret_new)

def setup_inputs(seed: int = 0) -> dict:
    key = jax.random.key(seed)
    ks = jax.random.split(key, 32)
    f32 = jnp.float32
    nrm = lambda k, shape, scale: jax.random.normal(k, shape, f32) * scale
    band_len = min(BAND, PAST_LEN)
    dt = jnp.exp(jax.random.uniform(ks[20], (DEPTH, H_A), f32, math.log(1e-3), math.log(1e-1)))
    return {
        "x_prompt": nrm(ks[0], (BATCH, SEQ, D_MODEL), 1.0),
        "x_sample": nrm(ks[1], (DEC_BATCH, DEC_SEQ, D_MODEL), 1.0),
        "state_gdn": nrm(ks[2], (DEPTH, DEC_BATCH, H_A, DK_A, DV_A), DK_A ** -0.5),
        "state_conv": nrm(ks[3], (DEPTH, DEC_BATCH, CONV_W - 1, CONV_DIM), 1.0),
        "cache_band_k": nrm(ks[4], (DEPTH, DEC_BATCH, band_len, H_B, DH_B), 1.0),
        "cache_band_v": nrm(ks[5], (DEPTH, DEC_BATCH, band_len, H_B, DH_B), 1.0),
        "state_ret": nrm(ks[6], (DEPTH, DEC_BATCH, H_C, DK_C, DV_C), 0.5),
        "norm_ffn1": 1.0 + nrm(ks[7], (DEPTH, D_MODEL), 0.02),
        "w_ffn1_gate": nrm(ks[8], (DEPTH, D_MODEL, D_FF), D_MODEL ** -0.5),
        "w_ffn1_up": nrm(ks[9], (DEPTH, D_MODEL, D_FF), D_MODEL ** -0.5),
        "w_ffn1_down": nrm(ks[10], (DEPTH, D_FF, D_MODEL), D_FF ** -0.5),
        "norm_mix": 1.0 + nrm(ks[11], (DEPTH, D_MODEL), 0.02),
        "w_in": nrm(ks[12], (DEPTH, D_MODEL, IN_COLS), D_MODEL ** -0.5),
        "conv_w": nrm(ks[13], (DEPTH, CONV_W, CONV_DIM), CONV_W ** -0.5),
        "a_log": jnp.log(jax.random.uniform(ks[14], (DEPTH, H_A), f32, 1.0, 16.0)),
        "dt_bias": dt + jnp.log(-jnp.expm1(-dt)),
        "gdn_norm": 1.0 + nrm(ks[15], (DEPTH, DV_A), 0.02),
        "rel_bias": nrm(ks[16], (DEPTH, H_B, 2 * REL_CLIP + 1), 0.1),
        "w_out": nrm(ks[17], (DEPTH, MIX, D_MODEL), MIX ** -0.5),
        "norm_ffn2": 1.0 + nrm(ks[18], (DEPTH, D_MODEL), 0.02),
        "w_ffn2_gate": nrm(ks[19], (DEPTH, D_MODEL, D_FF), D_MODEL ** -0.5),
        "w_ffn2_up": nrm(ks[21], (DEPTH, D_MODEL, D_FF), D_MODEL ** -0.5),
        "w_ffn2_down": nrm(ks[22], (DEPTH, D_FF, D_MODEL), D_FF ** -0.5),
        "norm_final": 1.0 + nrm(ks[23], (D_MODEL,), 0.02),
    }

def reference(x_prompt, x_sample, state_gdn, state_conv, cache_band_k, cache_band_v, state_ret,
              norm_ffn1, w_ffn1_gate, w_ffn1_up, w_ffn1_down, norm_mix, w_in, conv_w, a_log, dt_bias,
              gdn_norm, rel_bias, w_out, norm_ffn2, w_ffn2_gate, w_ffn2_up, w_ffn2_down, norm_final):

    def run(x, pos0, use_cache):
        B_ = x.shape[0]
        new = []
        for l in range(DEPTH):
            if use_cache:
                c = (state_conv[l], state_gdn[l], state_ret[l], cache_band_k[l], cache_band_v[l])
            else:
                c = (jnp.zeros((B_, CONV_W - 1, CONV_DIM), x.dtype),
                     jnp.zeros((B_, H_A, DK_A, DV_A), jnp.float32),
                     jnp.zeros((B_, H_C, DK_C, DV_C), jnp.float32), None, None)
            x = x + 0.5 * swiglu(rmsnorm(x, norm_ffn1[l]), w_ffn1_gate[l], w_ffn1_up[l], w_ffn1_down[l])
            m, st = token_mix(rmsnorm(x, norm_mix[l]), w_in[l], conv_w[l], a_log[l], dt_bias[l], gdn_norm[l],
                              rel_bias[l], w_out[l], c[0], c[1], c[2], c[3], c[4], pos0)
            x = x + m
            x = x + 0.5 * swiglu(rmsnorm(x, norm_ffn2[l]), w_ffn2_gate[l], w_ffn2_up[l], w_ffn2_down[l])
            new.append(st)
        y = rmsnorm(x, norm_final)
        g_, c_, k_, v_, r_ = zip(*new)
        return y, jnp.stack(g_), jnp.stack(c_), jnp.stack(k_), jnp.stack(v_), jnp.stack(r_)

    y_prompt, p_gdn, p_conv, p_band_k, p_band_v, p_ret = run(x_prompt, 0, False)
    y_sample, s_gdn, s_conv, s_band_k, s_band_v, s_ret = run(x_sample, PAST_LEN, True)
    return (y_prompt, y_sample, p_gdn, p_conv, p_band_k, p_band_v, p_ret,
            s_gdn, s_conv, s_band_k, s_band_v, s_ret)


_drawn_inputs = setup_inputs


def setup_inputs(seed=0):
    import zlib

    import numpy as np

    out = dict(_drawn_inputs(seed))
    spreads = {}
    factors = {'norm_ffn1': 3.756,
     'gdn_norm': 22.617,
     'rel_bias': 23.104,
     'norm_ffn2': 5.332,
     'norm_final': 8.48,
     'cache_band_k': 3.996,
     'cache_band_v': 3.036}
    for name, (base, spread) in spreads.items():
        noise = np.random.default_rng([zlib.crc32(name.encode()), seed]).standard_normal(out[name].shape)
        drawn = base * np.exp(spread * noise) if base else spread * noise
        out[name] = jnp.asarray(drawn.astype(out[name].dtype))
    for name, factor in factors.items():
        out[name] = (out[name] * factor).astype(out[name].dtype)
    return out
```

```python
from contextlib import ExitStack
import math

import numpy as np

import concourse.bass as bass
from concourse import mybir

F32 = mybir.dt.float32
F32R = mybir.dt.float32r
ACT = mybir.ActivationFunctionType
ALU = mybir.AluOpType
AX_X = mybir.AxisListType.X

P = 128
DEPTH, D_MODEL, D_FF = 2, 1024, 2816
SEQ, DEC = 256, 64
T = SEQ + DEC
PAST = 128
EPS = 1e-6
NEG = -1e30
KD = D_MODEL // P
KF = D_FF // P
NJ = KF // 2
H = 4
CONV_W, CONV_DIM = 4, 1536
CB = CONV_DIM // P
IN_COLS = 3848
TAIL0 = 2048
REL = 257
PAD = CONV_W - 1
UPW = PAD + SEQ + PAD + DEC
CW = UPW - PAD
TILES = [(0, 0, 128), (128, 128, 128), (256, 256 + PAD, 64)]

RAW, SPLIT = 4, 2
SLOT = 2048
DOWN_K = KF // 2
U_FFN = 2 * NJ + 2 * KD
U_FFN1, U_IN, U_OUT, U_FFN2 = 0, U_FFN, U_FFN + 16, U_FFN + 20
UNITS = 2 * U_FFN + 20
assert UNITS % RAW == 0

R_F1, R_MIX, R_F2, R_CONV, R_GDN, R_STATE, R_FINAL = 0, 8, 16, 24, 72, 73, 109
NPAR = 117
PAR_LOADS = 7

IN_UNITS = ([("conv", i, 256 * i) for i in range(4)] + [("tail", 0, TAIL0)]
            + [("conv", i, 256 * i) for i in (4, 5)]
            + [("kb", 0, 2312), ("qb", 0, 2056), ("vb", 0, 2568), ("z", 0, 1536), ("z", 1, 1792),
               ("qc", 0, 2824), ("kc", 0, 3080), ("vc", 0, 3336), ("gc", 0, 3592)])
CONV_UNIT = [0, 1, 2, 3, 5, 6]

LEVELS = {t: [s for s in (2, 4, 8, 16, 32, 64) if s < L] for t, (_, _, L) in enumerate(TILES)}


def mix_steps():
    def tile_steps(t):
        yield from (("vt", t), ("D", t), ("Bb", t), ("G", t), ("QK", t), ("kt", t), ("T1", t))
        for s in LEVELS[t]:
            yield ("Y", t, s)
            yield ("Z", t, s)
        if t:
            yield ("kS", t)
        yield from (("vn", t), ("o", t), ("Su", t), ("on", t))

    chain = [s for t in range(3) for s in tile_steps(t)]
    fill = [("unit", 8), ("unit", 9), ("btok", 0), ("btok", 1), ("btok", 2), ("bkc",), ("lc",)]
    for h in range(H):
        fill += [("sA", h), ("sB", h), ("pT", h), ("oB", h)]
        if h % 2:
            fill += [("unit", 10 + h // 2)]
    fill += [("zs",), ("unit", 12), ("unit", 13), ("rot", 0), ("rot", 1), ("unit", 14), ("rot", 2), ("rot", 3),
             ("unit", 15), ("gs",)]
    for t in range(3):
        fill += [("ctok", t), ("cqk", t), ("oC", t), ("R", t)]
    fill += [("cm", 0), ("cv", 0), ("cm", 1), ("cv", 1)]
    steps = [("unit", n) for n in range(7)] + [("ba",), ("unit", 7)] + [("ss", i) for i in range(8)] + [("dcol",)]
    done = 0
    for i, s in enumerate(chain):
        if s[0] == "on" and ("zs",) not in steps:
            while fill[done] != ("zs",):
                steps.append(fill[done])
                done += 1
            steps.append(fill[done])
            done += 1
        steps.append(s)
        while done < len(fill) and done * len(chain) < (i + 1) * len(fill):
            steps.append(fill[done])
            done += 1
    return steps + fill[done:]


STEPS = mix_steps()


def small_uses():
    yield ("par",)
    yield ("stat", 0)
    for s in STEPS:
        if s[0] == "Z":
            yield ("Zt",) + s[1:]
            if s[2] != LEVELS[s[1]][-1]:
                yield s
        elif s[0] not in ("unit", "zs", "gs"):
            yield s
    yield ("stat", 1)
    yield ("stat", 2)


NORMED = [s for s in STEPS if s[0] in ("on", "cv")]
LEVEL_DONE = {}
for _t in range(3):
    for _s in LEVELS[_t][:-1]:
        LEVEL_DONE[_t, _s] = len(LEVEL_DONE) + 1
assert STEPS.index(("bkc",)) < min(STEPS.index(("kS", 2)), STEPS.index(("oC", 2)))
assert STEPS.index(("oB", H - 1)) < STEPS.index(("unit", 12))
SQ0, SQ_OUT = (0, 12), 8
STORES = 10

USE = {key: (i % 4, i // 4) for i, key in enumerate(small_uses())}


def constants():
    i = np.arange(P)
    f = np.float32
    parts = {}
    parts["ident"] = np.eye(P, dtype=f)
    parts["ones"] = np.ones((P, P), f)
    parts["utri"] = (i[:, None] <= i[None, :]).astype(f)
    parts["future"] = np.where(i[:, None] <= i[None, :], 0, NEG).astype(f)
    for s in (1, 2, 4, 8, 16, 32, 64):
        j, q = i[:, None], i[None, :]
        parts[f"level{s}"] = ((j // (2 * s) == q // (2 * s)) & (j // s % 2 == 0) & (q // s % 2 == 1)).astype(f)
    rot = np.zeros((P, P), f)
    for m in range(P):
        if m % 64 < 32:
            rot[m + 32, m] = -1.0
        else:
            rot[m - 32, m] = 1.0
    parts["rot"] = rot
    parts["mean64"] = (i[:, None] // 64 == i[None, :] // 64).astype(f) / f(64)
    half = 32
    inv_freq = np.exp(f(-math.log(10000.0)) * np.arange(half, dtype=f) / f(half)).astype(f)
    pos = np.concatenate([np.arange(SEQ), PAST + np.arange(DEC)]).astype(f)
    ang = (inv_freq[i % 32][:, None] * pos[None, :]).astype(f)
    parts["cos"] = np.cos(ang).astype(f)
    parts["sin"] = np.sin(ang).astype(f)
    lg = np.log1p(-np.exp2(-5.0 - np.arange(H)))
    d = (i[None, :] - i[:, None])
    for h in range(H):
        parts[f"dmask{h}"] = np.where(d >= 0, np.exp(lg[h] * np.maximum(d, 0)) * 0.125, 0).astype(f)
    for b in range(2):
        parts[f"gq{b}"] = np.exp(lg[2 * b + i // 64][:, None] * (i[None, :] + 1.0)).astype(f)
    for L in (128, 64):
        parts[f"gk{L}"] = (np.exp(lg[None, :] * (L - 1.0 - i[:, None])) * 0.125).astype(f)
        parts[f"gl{L}"] = np.stack([np.exp(lg[2 * b + i // 64] * L) for b in range(2)], 1).astype(f)
    parts["eps"] = np.full((P, 1), EPS, f)
    parts["qscale"] = np.full((P, 1), -0.5 * math.log(128.0), f)
    at, n = {}, 0
    for k, v in parts.items():
        at[k] = (n, v.shape[1])
        n += v.shape[1]
    return np.concatenate(list(parts.values()), 1), at


def build(nc, x_prompt, x_sample, state_gdn, state_conv, cache_k, cache_v, state_ret, norm_ffn1, w_g1, w_u1, w_d1,
          norm_mix, w_in, conv_w, a_log, dt_bias, gdn_norm, rel_bias, w_out, norm_ffn2, w_g2, w_u2, w_d2,
          norm_final, consts, y_prompt, y_sample, p_gdn, p_conv, p_k, p_v, p_ret, s_gdn, s_conv, s_k, s_v, s_ret):
    _, CAT = constants()
    ctx = ExitStack()
    with ctx:
        def sb(name, shape, dt=F32):
            return ctx.enter_context(nc.sbuf_tensor(name, shape, dt))

        def sem(name):
            return ctx.enter_context(nc.semaphore(name))

        bias_copies = nc.dram_tensor("bias_copies", (P, H, 384), F32, kind="Internal")

        cst = sb("cst", [P, consts.shape[1]])
        xT = sb("xT", [P, KD, T])
        hh = sb("hh", [P, KD, T], F32R)
        hl = sb("hl", [P, KD, T], F32R)
        raw = sb("raw", [P, RAW, SLOT])
        whi = sb("whi", [P, SPLIT, SLOT], F32R)
        wlo = sb("wlo", [P, SPLIT, SLOT], F32R)
        tmp = sb("tmp", [P, 8, CW])
        rstd = sb("rstd", [P, T])
        parrow = sb("parrow", [NPAR, P])
        par = sb("par", [P, NPAR])
        bias = sb("bias", [P, H, 256])
        ck = sb("ck", [P, 256])
        cv = sb("cv", [P, 256])
        sS = sb("sS", [P, H, P])
        sR = sb("sR", [P, 2, 64])
        ea = sb("ea", [P, H])
        dtb = sb("dtb", [P, H])
        spare = sb("spare", [P, 5])

        with ExitStack() as ffn:
            act_hi = ffn.enter_context(nc.sbuf_tensor("act_hi", [P, KF, T], F32R))
            act_lo = ffn.enter_context(nc.sbuf_tensor("act_lo", [P, KF, T], F32R))
            gs = ffn.enter_context(nc.sbuf_tensor("gs", [P, 2, T], F32))
            prod = ffn.enter_context(nc.sbuf_tensor("prod", [P, 2, T], F32))
        with ExitStack() as ends:
            tok = ends.enter_context(nc.sbuf_tensor("tok", [P, 3, D_MODEL], F32))
        with ExitStack() as shared:
            up = shared.enter_context(nc.sbuf_tensor("up", [P, 4, UPW], F32))
        with ExitStack() as shared:
            z = shared.enter_context(nc.sbuf_tensor("z", [P, 4, T], F32))
        sb("up_rest", [P, 4 * UPW])
        qkv = sb("qkv", [P, CB, CW])
        bq = sb("bq", [P, 2, T])
        bk = sb("bk", [P, 2, T])
        bv = sb("bv", [P, 2, T])
        gc = sb("gc", [P, 2, T])
        lastc = sb("lastc", [P, 2, PAD, CB])
        lastr = parrow[0:2 * PAD * CB, :]
        baT = sb("baT", [8, T])
        bac = sb("bac", [P, 3, 8])
        gt = sb("gt", [P, 8, 3, H])
        GX, AX, RX, G, BETA, ND, ED, NBE = range(8)
        ug = sb("ug", [P, H, P])
        bi = sb("bi", [P, H, P])
        rn = sb("rn", [P, 2, CW])
        vb = sb("vb", [P, H, P])
        kt = sb("kt", [P, H, P])
        lm = sb("lm", [P, H, P])
        eD = sb("eD", [P, H, P])
        edl = sb("edl", [P, H])
        aT = sb("aT", [P, H, P])
        U = sb("U", [P, H, P])
        Us = sb("Us", [P, H, P])
        Vt = sb("Vt", [P, H, P])
        Vn = sb("Vn", [P, H, P])
        Ysb = sb("Ysb", [P, H, P])
        vn = sb("vn", [P, H, P])
        pS = sb("pS", [P, H, P])
        pR = sb("pR", [P, 2, 64])
        prob = sb("prob", [P, 2 * T])
        mx = sb("mx", [P, 3, 3])
        pT = sb("pT", [P, 512])
        btk = sb("btk", [P, 3, 256])
        btv = sb("btv", [P, 3, 256])
        kcT = sb("kcT", [P, 2, P])
        ctk, ctv = ck, cv
        aC = pT[:, :].rearrange("p (h l) -> p h l", h=H)
        oC = prob[:, :].rearrange("p (b l) -> p b l", b=2)
        osq = sb("osq", [P, 512])
        rsc = sb("rsc", [P, T])
        rno = sb("rno", [P, 512])

        psum = ctx.enter_context(nc.psum_tensor("psum", [P, 8, 512], F32))

        def C(name, rows=P, cols=None):
            at, n = CAT[name]
            return cst[0:rows, at:at + (cols or n)]

        landed = [sem(f"landed{i}") for i in range(RAW)]
        hi_done = sem("hi_done")
        lo_done = sem("lo_done")
        unit_used = sem("unit_used")
        par_loaded = sem("par_loaded")
        gate_loaded = sem("gate_loaded")
        state_loaded = sem("state_loaded")
        cache_loaded = sem("cache_loaded")
        row_loaded = sem("row_loaded")
        copies_stored = sem("copies_stored")
        bias_loaded = sem("bias_loaded")
        stored = sem("stored")
        layer_open = sem("layer_open")
        arrived = sem("arrived")
        names = ("gate_silu product act_hi_done act_lo_done x_updated sq_done rstd_done hf_done hh_done hl_done "
                 "unit_out conv_done silu_done sq2_done rn_done qk_normed gates_in gates_act gates_done spread ed_done "
                 "eD_done lm_done tri_done level_done qs_done z_done gc_done gn_done gated maxima exps probs "
                 "rope_done upper_half qd_done oc_sq bias_masked opening act_step dve_step pool_step").split()
        S = {n: sem(n) for n in names}
        filled = [sem(f"filled{i}") for i in range(4)]
        drained = [sem(f"drained{i}") for i in range(4)]
        for n in ("y_normed", "y_turned", "y_out", "y_stored"):
            S[n] = sem(n)
        cleared = [*map(S.get, names), *filled, *drained]
        first_load = sem("first_load")
        x_turned = sem("x_turned")
        x_in = sem("x_in")

        def small(key):
            return psum[:, 4 + USE[key][0], :]

        def open_bank(pe, key):
            k, n = USE[key]
            if n:
                pe.wait_ge(drained[k], n)

        def fill(ins, key):
            ins.then_inc(filled[USE[key][0]], 1)

        def wait_filled(eng, key):
            k, n = USE[key]
            eng.wait_ge(filled[k], n + 1)

        def wait_drained(eng, key):
            k, n = USE[key]
            eng.wait_ge(drained[k], n + 1)

        class Engine:

            def __init__(self, eng, step):
                self.eng, self.step, self.counts = eng, step, {}

            def do(self, ins, name=None):
                name = name or self.step
                self.counts[name] = self.counts.get(name, 0) + 1
                ins.then_inc(S[name], 1)
                self.eng.wait_ge(S[name], self.counts[name])

            def drain(self, ins, key):
                k, n = USE[key]
                ins.then_inc(drained[k], 1)
                self.eng.wait_ge(drained[k], n + 1)

            def do_at(self, ins, s, value):
                ins.then_inc(s, 1)
                self.eng.wait_ge(s, value)

        def in_turn(eng, first, blocks, last, body):
            for n in range(first):
                body(n, 0)
            assert (blocks - first - last) % 2 == 0
            with eng.Fori(0, (blocks - first - last) // 2) as i:
                body(first, i)
                body(first + 1, i)
            for n in range(blocks - last, blocks):
                body(n, 0)

        block = ctx.enter_context(nc.Block())

        @block.sync
        def _(sp):
            def load(layer, u, i, src):
                sp.wait_ge(lo_done, layer * UNITS + 4 * i + u + 1)
                n = src.shape[1] * src.shape[2]
                dst = raw[:, u % RAW, 0:n].rearrange("p (k c) -> p k c", k=src.shape[1])
                sp.dma_start(dst, src).then_inc(landed[u % RAW], 16)

            def view(w, layer, row0, rows, col, cols):
                return w[bass.ds(layer, 1), row0:row0 + rows, bass.ds(col, cols)].rearrange(
                    "a (k p) c -> p (a k) c", p=P)

            def ffn_units(layer, u0, wg, wu, wd):
                def gate_up(j, i):
                    u = u0 + 2 * j
                    load(layer, u, i, view(wg, layer, 0, D_MODEL, (2 * i + j) * 256, 256))
                    load(layer, u + 1, i, view(wu, layer, 0, D_MODEL, (2 * i + j) * 256, 256))

                def down(b, i):
                    u = u0 + 2 * NJ + 2 * b
                    for r in range(2):
                        load(layer, u + r, i, view(wd, layer, r * DOWN_K * P, DOWN_K * P, (2 * i + b) * P, P))

                in_turn(sp, 1, NJ, 0, gate_up)
                in_turn(sp, 2, KD, 2, down)

            with sp.Fori(0, DEPTH) as layer:
                ffn_units(layer, U_FFN1, w_g1, w_u1, w_d1)
                for n, (kind, _, col) in enumerate(IN_UNITS):
                    load(layer, U_IN + n, 0, view(w_in, layer, 0, D_MODEL, col, P if kind == "tail" else 256))
                for d in range(4):
                    load(layer, U_OUT + d, 0, view(w_out, layer, 0, D_MODEL, d * 256, 256))
                ffn_units(layer, U_FFN2, w_g2, w_u2, w_d2)

        @block.gpsimd
        def _(pool):
            pool.dma_start(cst[:, :], consts).then_inc(first_load, 16)
            pool.dma_start(tok[:, 0:2, :], x_prompt[0].rearrange("(t p) d -> p t d", p=P)).then_inc(first_load, 16)
            pool.dma_start(tok[0:DEC, 2, :], x_sample[0]).then_inc(first_load, 16)
            pool.memset(spare[:, 3:4], 0.0).then_inc(lo_done, RAW)
            pool.wait_ge(lo_done, RAW)
            pool.memset(spare[:, 4:5], 0.0).then_inc(unit_used, SPLIT)
            pool.wait_ge(unit_used, SPLIT)

            def idle(n):
                return pool.tensor_tensor(spare[:, n:n + 1], C("eps"), C("eps"), ALU.add)

            pool.wait_ge(first_load, 48)

            with pool.Fori(0, DEPTH) as layer:
                pool.wait_ge(arrived, 3 * layer + 3)
                idle(0).then_inc(S["opening"], 1)
                pool.wait_ge(S["opening"], 1)
                for s in cleared:
                    pool.sem_clear(s)
                pool.memset(spare[:, 2:3], 0.0).then_inc(layer_open, 1)
                me = Engine(pool, "pool_step")

                def rows(w, n):
                    return w[bass.ds(layer, 1)].rearrange("a (b p) -> (a b) p", p=P)

                for w, at, n in ((norm_ffn1, R_F1, 8), (norm_mix, R_MIX, 8), (norm_ffn2, R_F2, 8), (gdn_norm, R_GDN, 1)):
                    pool.dma_start(parrow[at:at + n, :], rows(w, n)).then_inc(par_loaded, 16)
                pool.dma_start(parrow[R_CONV:R_CONV + 4 * CB, :],
                               conv_w[bass.ds(layer, 1)].rearrange("a j (b p) -> (a j b) p", p=P)
                               ).then_inc(par_loaded, 16)
                pool.dma_start(parrow[R_STATE:R_STATE + PAD * CB, :],
                               state_conv[bass.ds(layer, 1)].rearrange("a e j (b p) -> (a e j b) p", p=P)
                               ).then_inc(par_loaded, 16)
                pool.dma_start(parrow[R_FINAL:R_FINAL + 8, :], norm_final.rearrange("(b p) -> b p", p=P)
                               ).then_inc(par_loaded, 16)
                for w, dst in ((a_log, ea), (dt_bias, dtb)):
                    pool.dma_start(dst[:, :], w[bass.ds(layer, 1)].to_broadcast([P, H])).then_inc(gate_loaded, 16)
                pool.dma_start(sS[:, :, :], state_gdn[bass.ds(layer, 1)].rearrange("a e h k v -> k (a e h) v")
                               ).then_inc(state_loaded, 16)
                pool.dma_start(sR[:, :, :], state_ret[bass.ds(layer, 1)].rearrange("a e (b c) k v -> (a e c k) b v", c=2)
                               ).then_inc(state_loaded, 16)
                for w, dst in ((cache_k, ck), (cache_v, cv)):
                    pool.dma_start(dst[:, :], w[bass.ds(layer, 1)].rearrange("a e t h d -> (a e t) (h d)")
                                   ).then_inc(cache_loaded, 16)
                row = bias[0:H, :, :].rearrange("p h x -> p (h x)")[:, 0:384]
                pool.dma_start(row[:, P:384], rel_bias[bass.ds(layer, 1), :, 0:256].rearrange("a h o -> (a h) o")
                               ).then_inc(row_loaded, 16)
                pool.wait_ge(row_loaded, (layer + 1) * 16)
                me.do(idle(1))
                me.do(pool.tensor_scalar(row[:, 0:P], C("ones", H), row[:, P:P + 1], None, ALU.mult))
                pool.dma_start(bias_copies.rearrange("p h x -> h p x"), row[:, None, :].to_broadcast([H, P, 384])
                               ).then_inc(copies_stored, 16)
                pool.wait_ge(copies_stored, (layer + 1) * 16)
                me.do(idle(1))
                pool.dma_start(bias[:, :, :], bass.AP(bias_copies, P, [[H * 384 - 1, P], [384, H], [1, 256]])
                               ).then_inc(bias_loaded, 16)
                pool.wait_ge(bias_loaded, (layer + 1) * 16)
                me.do(idle(1))
                me.do(pool.memset(bias[0:64, :, 192:256], NEG), "bias_masked")

                stores = 0

                def store(dst, src):
                    nonlocal stores
                    pool.dma_start(dst, src).then_inc(stored, 16)
                    stores += 16

                one = bass.ds(layer, 1)
                for step in STEPS:
                    if step[0] == "D":
                        t = step[1]
                        L = TILES[t][2]
                        if t == 0:
                            pool.wait_ge(S["gates_done"], 1)
                        else:
                            wait_drained(pool, ("Bb", t - 1))
                        for h in range(H):
                            me.do(pool.tensor_scalar(ug[0:L, h, 0:L], C("utri", L, L), gt[0:L, G, t, h:h + 1], None,
                                                     ALU.mult))
                            me.do(pool.tensor_scalar(bi[0:L, h, 0:L], C("ident", L, L), gt[0:L, BETA, t, h:h + 1],
                                                     None, ALU.mult), "spread" if h == H - 1 else None)
                    elif step == ("btok", 2):
                        wait_drained(pool, step)
                        for w, src in ((p_k, btk), (p_v, btv)):
                            store(w[one].rearrange("a e (t p) h d -> p (a e t) (h d)", p=P), src[:, 0:2, :])
                        for w, src in ((s_k, btk), (s_v, btv)):
                            store(w[one].rearrange("a e p h d -> (a e p) (h d)"), src[0:DEC, 2, :])
                    elif step[0] == "lc":
                        wait_drained(pool, step)
                        for s, w in enumerate((p_conv, s_conv)):
                            store(w[one].rearrange("a e r (b p) -> (a e r b) p", p=P),
                                  lastr[s * PAD * CB:(s + 1) * PAD * CB, :])
                    elif step in (("Su", 1), ("Su", 2)):
                        wait_drained(pool, step)
                        store((p_gdn if step[1] == 1 else s_gdn)[one].rearrange("a e h k v -> k (a e h) v"),
                              (pS if step[1] == 1 else sS)[:, :, :])
                    elif step in (("R", 1), ("R", 2)):
                        wait_drained(pool, step)
                        store((p_ret if step[1] == 1 else s_ret)[one].rearrange("a e (b c) k v -> (a e c k) b v", c=2),
                              (pR if step[1] == 1 else sR)[:, :, :])
                assert stores == 16 * STORES
                pool.wait_ge(stored, (layer + 1) * stores)
                me.do(idle(1))
            for t in range(3):
                pool.wait_ge(S["y_out"], 2 * t + 2)
                if t < 2:
                    pool.dma_start(y_prompt[0, t * P:(t + 1) * P, :], tok[:, t, :]).then_inc(S["y_stored"], 16)
                else:
                    pool.dma_start(y_sample[0], tok[0:DEC, 2, :]).then_inc(S["y_stored"], 16)
            pool.wait_ge(S["y_stored"], 48)

        @block.tensor
        def _(pe):
            def products(layer, u, i, nk, nb, hi, lo, banks, k0=0, start=True, stop=True, before=None):
                pe.wait_ge(lo_done, layer * UNITS + 4 * i + u + 1 + RAW)
                s, width = u % SPLIT, nb * P
                for b in range(nb):
                    out = psum[:, banks[b], 0:T]
                    for k in range(nk):
                        if before and b == 0:
                            before(k)
                        at = k * width + b * P
                        wh, wl = whi[:, s, at:at + P], wlo[:, s, at:at + P]
                        pe.matmul(out, wh, hi[:, k0 + k, :], start=start and k == 0, stop=False)
                        pe.matmul(out, wh, lo[:, k0 + k, :], start=False, stop=False)
                        mm = pe.matmul(out, wl, hi[:, k0 + k, :], start=False, stop=stop and k == nk - 1)
                mm.then_inc(unit_used, 1)

            def input_ready(norm):
                return lambda k: pe.wait_ge(S["hl_done"], norm * KD + k + 1)

            def ffn_products(layer, u0, f, norm):
                def gate_up(n, i):
                    u = u0 + 2 * n
                    if n:
                        pe.wait_ge(S["gate_silu"], NJ * f + 2 * i + n)
                    products(layer, u, i, KD, 2, hh, hl, (0, 1), before=None if n else input_ready(norm))
                    if n:
                        pe.wait_ge(S["product"], NJ * f + 2 * i + n)
                    products(layer, u + 1, i, KD, 2, hh, hl, (2, 3))

                def act_ready(k0):
                    return lambda k: pe.wait_ge(S["act_lo_done"], NJ * f + (k0 + k) // 2 + 1)

                def add_squares(n, i, last=False):
                    if n == 0:
                        open_bank(pe, stat)
                    pe.wait_ge(S["sq_done"], SQ0[f] + 2 * i + n + 1)
                    block = tmp[:, bass.ds(2 * i + n, 1), 0:T].rearrange("p a t -> p (a t)")
                    mm = pe.matmul(small(stat)[:, 0:T], C("ones"), block, start=n == 0, stop=last)
                    if last:
                        fill(mm, stat)

                def down(n, i):
                    u = u0 + 2 * NJ + 2 * n
                    if n == 0:
                        pe.wait_ge(S["gate_silu"], NJ * f + NJ)
                    products(layer, u, i, DOWN_K, 1, act_hi, act_lo, (n % 2,), stop=False,
                             before=None if n else act_ready(0))
                    if n:
                        add_squares(n - 1, i)
                    products(layer, u + 1, i, DOWN_K, 1, act_hi, act_lo, (n % 2,), k0=DOWN_K, start=False,
                             before=None if n else act_ready(DOWN_K))

                stat = ("stat", 2 * f)
                in_turn(pe, 1, NJ, 0, gate_up)
                in_turn(pe, 2, KD, 2, down)
                add_squares(KD - 1, 0, last=True)

            def heads(key, L, width, lhs, rhs):
                bank = small(key)
                for h in range(H):
                    mm = pe.matmul(bank[0:L, h * width:(h + 1) * width], lhs(h), rhs(h), start=True, stop=True)
                fill(mm, key)

            def turn(out, src):
                n = src.shape[0]
                return pe.transpose(out, src, C("ident", n, n))

            pe.wait_ge(first_load, 48)
            for k in range(KD):
                for t, (c0, _, L) in enumerate(TILES):
                    mm = turn(psum[:, k, c0:c0 + L], tok[0:L, t, k * P:(k + 1) * P])
                mm.then_inc(x_turned, 1)
            pe.wait_ge(x_in, 2 * KD)
            for k in range(KD):
                pe.wait_ge(x_in, 2 * k + 2)
                mm = pe.matmul(psum[:, 4, 0:T], C("ones"), tmp[:, k, 0:T], start=k == 0, stop=k == KD - 1)
            mm.then_inc(x_turned, 1)

            with pe.Fori(0, DEPTH) as layer:
                pe.drain().then_inc(arrived, 1)
                pe.wait_ge(layer_open, layer + 1)
                pe.wait_ge(par_loaded, (layer + 1) * PAR_LOADS * 16)
                open_bank(pe, ("par",))
                fill(turn(small(("par",))[:, 0:NPAR], parrow[:, :]), ("par",))
                ffn_products(layer, U_FFN1, 0, 0)

                for step in STEPS:
                    kind, t = step[0], (step[1] if len(step) > 1 else None)
                    if kind == "unit":
                        if t >= 2:
                            pe.wait_ge(S["unit_out"], t - 1)
                        nb = 1 if IN_UNITS[t][0] == "tail" else 2
                        products(layer, U_IN + t, 0, KD, nb, hh, hl, (2 * (t % 2), 2 * (t % 2) + 1),
                                 before=None if t else input_ready(1))
                        continue
                    if kind in ("zs", "gs"):
                        continue
                    if kind != "Z":
                        open_bank(pe, step)
                        bank = small(step)
                    if kind not in ("ba", "ss", "dcol", "bkc", "lc", "sA", "sB", "pT", "oB", "rot", "cm", "cv"):
                        c0, p0, L = TILES[t]
                        q = lambda h: qkv[:, h, p0:p0 + L]
                        k = lambda h: qkv[:, H + h, p0:p0 + L]
                        state, rstate = (pS, pR) if t < 2 else (sS, sR)
                    if kind in ("sA", "sB", "pT", "oB"):
                        b, r = t // 2, slice(64 * (t % 2), 64 * (t % 2) + 64)
                    if kind == "ba":
                        pe.wait_ge(S["unit_out"], 5)
                        for n, (c0, _, L) in enumerate(TILES):
                            mm = turn(bank[0:L, 8 * n:8 * n + 8], baT[:, c0:c0 + L])
                        fill(mm, step)
                    elif kind == "ss":
                        pe.wait_ge(S["sq2_done"], t + 1)
                        fill(pe.matmul(bank[:, 0:CW], C("ones"), tmp[:, t, :], start=True, stop=True), step)
                    elif kind == "dcol":
                        pe.wait_ge(S["gates_done"], 1)
                        for n, (_, _, L) in enumerate(TILES):
                            mm = pe.matmul(bank[0:L, H * n:H * n + H], C("utri", L, L), gt[0:L, G, n, :],
                                           start=True, stop=True)
                        fill(mm, step)
                    elif kind == "vt":
                        pe.wait_ge(S["silu_done"], 6)
                        for h in range(H):
                            mm = turn(bank[0:L, h * P:(h + 1) * P], qkv[:, 2 * H + h, p0:p0 + L])
                        fill(mm, step)
                    elif kind == "D":
                        pe.wait_ge(S["spread"], t + 1)
                        fill(pe.matmul(bank[:, 0:H * L].rearrange("p (h l) -> p h l", h=H), C("ones", L),
                                       ug[0:L, :, 0:L], start=True, stop=True), step)
                    elif kind == "Bb":
                        fill(pe.matmul(bank[0:L, 0:H * L].rearrange("p (h l) -> p h l", h=H), C("ones", L, L),
                                       bi[0:L, :, 0:L], start=True, stop=True), step)
                    elif kind == "G":
                        pe.wait_ge(S["qk_normed"], 8)
                        heads(step, L, L, k, k)
                    elif kind == "QK":
                        heads(step, L, L, k, q)
                    elif kind == "kt":
                        for h in range(H):
                            mm = turn(bank[0:L, h * P:(h + 1) * P], k(h))
                        fill(mm, step)
                    elif kind == "T1":
                        pe.wait_ge(S["tri_done"], t + 1)
                        for h in range(H):
                            mm = turn(bank[0:L, h * L:(h + 1) * L], Vt[0:L, h, 0:L])
                        fill(mm, step)
                    elif kind == "Y":
                        s = step[2]
                        if s == LEVELS[t][0]:
                            wait_drained(pe, ("T1", t))
                        else:
                            pe.wait_ge(S["level_done"], LEVEL_DONE[t, s // 2])
                        heads(step, L, L, lambda h: Us[0:L, h, 0:L], lambda h: Vn[0:L, h, 0:L])
                    elif kind == "Z":
                        s = step[2]
                        wait_drained(pe, ("Y", t, s))
                        open_bank(pe, ("Zt", t, s))
                        heads(("Zt", t, s), L, L, lambda h: Ysb[0:L, h, 0:L], lambda h: Vt[0:L, h, 0:L])
                        if s != LEVELS[t][-1]:
                            open_bank(pe, step)
                            heads(step, L, L, lambda h: Vt[0:L, h, 0:L], lambda h: Ysb[0:L, h, 0:L])
                    elif kind == "kS":
                        heads(step, L, P, k, lambda h: state[:, h, :])
                    elif kind == "vn":
                        wait_drained(pe, ("Zt", t, LEVELS[t][-1]))
                        wait_drained(pe, ("kS", t) if t else ("vt", t))
                        heads(step, L, P, lambda h: Vt[0:L, h, 0:L], lambda h: vb[0:L, h, :])
                    elif kind == "o":
                        wait_drained(pe, ("vn", t))
                        if t:
                            pe.wait_ge(S["qs_done"], t)
                        for h in range(H):
                            if t:
                                pe.matmul(bank[:, h * L:(h + 1) * L], state[:, h, :], q(h), start=True, stop=False)
                            mm = pe.matmul(bank[:, h * L:(h + 1) * L], vn[0:L, h, :], aT[0:L, h, 0:L],
                                           start=t == 0, stop=True)
                        fill(mm, step)
                    elif kind == "Su":
                        wait_drained(pe, ("kt", t))
                        heads(step, P, P, lambda h: kt[0:L, h, :], lambda h: vn[0:L, h, :])
                    elif kind == "on":
                        wait_drained(pe, ("o", t))
                        fill(pe.matmul(bank[:, 0:H * L], C("ones"), osq[:, 0:H * L], start=True, stop=True), step)
                    elif kind == "btok":
                        pe.wait_ge(S["unit_out"], 10)
                        for b in range(2):
                            turn(bank[0:L, b * P:(b + 1) * P], bk[:, b, c0:c0 + L])
                            mm = turn(bank[0:L, 256 + b * P:256 + (b + 1) * P], bv[:, b, c0:c0 + L])
                        fill(mm, step)
                    elif kind == "bkc":
                        pe.wait_ge(cache_loaded, (layer + 1) * 32)
                        pe.wait_ge(state_loaded, (layer + 1) * 32)
                        for b in range(2):
                            mm = turn(bank[:, b * P:(b + 1) * P], ck[:, b * P:(b + 1) * P])
                        fill(mm, step)
                    elif kind == "lc":
                        pe.wait_ge(S["conv_done"], 6)
                        fill(turn(bank[0:2 * PAD * CB, 0:P], lastc[:, :, :, :].rearrange("p s r b -> p (s r b)")), step)
                    elif kind == "sA":
                        pe.matmul(bank[:, 0:P], bq[r, b, 0:P], bk[r, b, 0:P], start=True, stop=True)
                        fill(pe.matmul(bank[:, P:3 * P], bq[r, b, P:2 * P], bk[r, b, 0:2 * P], start=True, stop=True), step)
                    elif kind == "sB":
                        wait_drained(pe, ("bkc",))
                        pe.matmul(bank[0:DEC, 0:P], bq[r, b, SEQ:T], kcT[r, b, :], start=True, stop=True)
                        fill(pe.matmul(bank[0:DEC, P:P + DEC], bq[r, b, SEQ:T], bk[r, b, SEQ:T], start=True, stop=True),
                             step)
                    elif kind == "pT":
                        pe.wait_ge(S["probs"], t + 1)
                        for n in range(3):
                            turn(bank[:, n * P:(n + 1) * P], prob[:, n * P:(n + 1) * P])
                        turn(bank[:, 384:448], prob[0:DEC, 384:512])
                        fill(turn(bank[0:DEC, 448:512], prob[0:DEC, 512:576]), step)
                    elif kind == "oB":
                        wait_drained(pe, ("pT", t))
                        wait_drained(pe, ("btok", 2))
                        v = slice(64 * t, 64 * t + 64)
                        pe.matmul(bank[r, 0:128], btv[:, 0, v], pT[:, 0:128], start=True, stop=True)
                        pe.matmul(bank[r, 128:256], btv[:, 0, v], pT[:, 128:256], start=True, stop=False)
                        pe.matmul(bank[r, 128:256], btv[:, 1, v], pT[:, 256:384], start=False, stop=True)
                        pe.matmul(bank[r, 256:320], cv[:, v], pT[:, 384:448], start=True, stop=False)
                        fill(pe.matmul(bank[r, 256:320], btv[0:DEC, 2, v], pT[0:DEC, 448:512], start=False, stop=True), step)
                    elif kind == "rot":
                        pe.wait_ge(S["unit_out"], 13 + t // 2)
                        fill(pe.matmul(bank[:, 0:T], C("rot"), (bq, bk)[t // 2][:, t % 2, :], start=True, stop=True), step)
                    elif kind == "ctok":
                        pe.wait_ge(S["rope_done"], 4)
                        pe.wait_ge(S["unit_out"], 15)
                        for b in range(2):
                            turn(bank[0:L, b * P:(b + 1) * P], bk[:, b, c0:c0 + L])
                            mm = turn(bank[0:L, 256 + b * P:256 + (b + 1) * P], bv[:, b, c0:c0 + L])
                        fill(mm, step)
                    elif kind == "cqk":
                        for h in (0, 2, 1, 3):
                            b, r = h // 2, slice(64 * (h % 2), 64 * (h % 2) + 64)
                            mm = pe.matmul(bank[0:L, h * L:(h + 1) * L], bk[r, b, c0:c0 + L], bq[r, b, c0:c0 + L],
                                           start=True, stop=True)
                            if h == 2:
                                mm.then_inc(S["upper_half"], 1)
                                pe.wait_ge(S["upper_half"], t + 1)
                        fill(mm, step)
                    elif kind == "oC":
                        wait_drained(pe, ("cqk", t))
                        wait_drained(pe, ("ctok", t))
                        if t:
                            pe.wait_ge(S["qd_done"], t)
                            wait_drained(pe, ("R", t - 1))
                        for h in range(H):
                            b, r = h // 2, slice(64 * (h % 2), 64 * (h % 2) + 64)
                            out = bank[r, b * P:b * P + L]
                            if t:
                                pe.matmul(out, rstate[r, b, :], bq[r, b, c0:c0 + L], start=True, stop=False)
                            mm = pe.matmul(out, ctv[:, 64 * h:64 * h + 64], aC[:, h, 0:L], start=t == 0, stop=True)
                        fill(mm, step)
                    elif kind == "R":
                        for h in range(H):
                            b, r = h // 2, slice(64 * (h % 2), 64 * (h % 2) + 64)
                            v = slice(64 * h, 64 * h + 64)
                            mm = pe.matmul(bank[r, b * 64:b * 64 + 64], ctk[0:L, v], ctv[0:L, v], start=True, stop=True)
                        fill(mm, step)
                    elif kind == "cm":
                        wait_drained(pe, ("oC", 2))
                        fill(pe.matmul(bank[:, 0:T], C("mean64"), oC[:, t, :], start=True, stop=True), step)
                    elif kind == "cv":
                        pe.wait_ge(S["oc_sq"], t + 1)
                        fill(pe.matmul(bank[:, 0:T], C("mean64"), rsc[:, :], start=True, stop=True), step)

                stat = ("stat", 1)

                def pair_squares(d):
                    if d == 0:
                        open_bank(pe, stat)
                    pe.wait_ge(S["sq_done"], SQ_OUT + d + 1)
                    for b in (2 * d, 2 * d + 1):
                        mm = pe.matmul(small(stat)[:, 0:T], C("ones"), tmp[:, b, 0:T], start=b == 0, stop=b == KD - 1)
                    if d == 3:
                        fill(mm, stat)

                for d in range(4):
                    products(layer, U_OUT + d, 0, KD, 2, hh, hl, (2 * (d % 2), 2 * (d % 2) + 1),
                             before=None if d else input_ready(2))
                    if d:
                        pair_squares(d - 1)
                pair_squares(3)
                ffn_products(layer, U_FFN2, 1, 3)

            pe.wait_ge(S["y_normed"], KD)
            for t, (c0, _, L) in enumerate(TILES):
                for half in range(2):
                    for n in range(4):
                        mm = turn(psum[0:L, 2 * t + half, n * P:(n + 1) * P], tmp[:, 4 * half + n, c0:c0 + L])
                    mm.then_inc(S["y_turned"], 1)

        @block.scalar
        def _(act):
            A = act.activation

            def split_hi(layer, u, i=0, width=SLOT):
                act.wait_ge(landed[u % RAW], (layer * (UNITS // RAW) + i + u // RAW + 1) * 16)
                act.wait_ge(unit_used, layer * UNITS + 4 * i + u + 1)
                ins = A(whi[:, u % SPLIT, 0:width], raw[:, u % RAW, 0:width], ACT.Copy)
                ins.then_inc(hi_done, 1)
                act.wait_ge(hi_done, layer * UNITS + 4 * i + u + 1)

            def wait_products(layer, u, i=0):
                act.wait_ge(unit_used, layer * UNITS + 4 * i + u + 1 + SPLIT)

            def rsqrt(dst, src, scale, me, key, name, extra=0.0):
                me.drain(A(dst, src, ACT.Ln, bias=C("eps"), scale=scale), key)
                me.do(A(dst, dst, ACT.Exp, bias=extra, scale=-0.5), name)

            def ffn(layer, u0, f, norm, me):
                def gate_up(n, i):
                    u = u0 + 2 * n
                    at = bass.ds(2 * (2 * i + n), 2)
                    split_hi(layer, u + 1, i)
                    wait_products(layer, u, i)
                    if n:
                        act.wait_ge(S["product"], NJ * f + 2 * i + n)
                    me.do_at(A(gs[:, :, :], psum[:, 0:2, 0:T], ACT.Silu), S["gate_silu"], NJ * f + 2 * i + n + 1)
                    split_hi(layer, u + 2, i)
                    act.wait_ge(S["product"], NJ * f + 2 * i + n + 1)
                    me.do_at(A(act_hi[:, at, :], prod[:, :, :], ACT.Copy), S["act_hi_done"], NJ * f + 2 * i + n + 1)

                def down(n, i):
                    u = u0 + 2 * NJ + 2 * n
                    for r in range(2):
                        if u + r + 1 < UNITS:
                            split_hi(layer, u + r + 1, i, SLOT if n == KD - 1 and r else DOWN_K * P)
                    act.wait_ge(S["x_updated"], SQ0[f] + 2 * i + n + 1)
                    at = bass.ds(2 * i + n, 1)
                    me.do_at(A(tmp[:, at, 0:T], xT[:, at, :], ACT.Square), S["sq_done"], SQ0[f] + 2 * i + n + 1)

                in_turn(act, 1, NJ, 0, gate_up)
                in_turn(act, 2, KD, 2, down)

            def apply_norm(norm, hf, me):
                for k in range(KD):
                    act.wait_ge(S["hf_done"], hf * KD + k + 1)
                    me.do(A(hh[:, k, :], tmp[:, k, 0:T], ACT.Copy), "hh_done")

            def statistics(i, me):
                key = ("stat", i)
                wait_filled(act, key)
                rsqrt(rstd[:, :], small(key)[:, 0:T], 1.0 / D_MODEL, me, key, "rstd_done")

            act.wait_ge(first_load, 48)
            n = 0
            for k in range(KD):
                act.wait_ge(x_turned, k + 1)
                for dst, src, f in ((xT[:, k, :], psum[:, k, 0:T], ACT.Copy), (tmp[:, k, 0:T], xT[:, k, :], ACT.Square)):
                    A(dst, src, f).then_inc(x_in, 1)
                    n += 1
                    act.wait_ge(x_in, n)
            act.wait_ge(x_turned, KD + 1)
            A(rstd[:, :], psum[:, 4, 0:T], ACT.Ln, bias=C("eps"), scale=1.0 / D_MODEL).then_inc(x_in, 1)
            act.wait_ge(x_in, n + 1)
            A(rstd[:, :], rstd[:, :], ACT.Exp, scale=-0.5).then_inc(x_in, 1)
            act.wait_ge(x_in, n + 2)

            with act.Fori(0, DEPTH) as layer:
                act.drain().then_inc(arrived, 1)
                act.wait_ge(layer_open, layer + 1)
                me = Engine(act, "act_step")
                split_hi(layer, 0)
                apply_norm(0, 0, me)
                ffn(layer, U_FFN1, 0, 0, me)
                statistics(0, me)
                apply_norm(1, 1, me)

                silu_pairs = 0

                def conv_silu():
                    nonlocal silu_pairs
                    act.wait_ge(S["conv_done"], silu_pairs + 1)
                    pair = qkv[:, 2 * silu_pairs:2 * silu_pairs + 2, :]
                    me.do(A(pair, pair, ACT.Silu), "silu_done")
                    silu_pairs += 1

                for step in STEPS:
                    kind, t = step[0], (step[1] if len(step) > 1 else None)
                    if kind not in ("unit", "zs", "gs", "ba", "ss", "dcol", "bkc", "lc", "sA", "sB", "pT", "oB", "rot",
                                    "cm", "cv"):
                        c0, p0, L = TILES[t]
                        wide = lambda x: x[:, 0:H * L].rearrange("p (h l) -> p h l", h=H)
                    if kind == "unit":
                        if t < 15:
                            split_hi(layer, U_IN + t + 1, 0, KD * P if IN_UNITS[t + 1][0] == "tail" else SLOT)
                        else:
                            split_hi(layer, U_OUT)
                        if t < 7 and t - 1 in CONV_UNIT:
                            conv_silu()
                        wait_products(layer, U_IN + t)
                        what, i, _ = IN_UNITS[t]
                        src = psum[:, 2 * (t % 2):2 * (t % 2) + 2, 0:T]
                        if what == "conv":
                            slot = 2 * (i % 2)
                            if i >= 2:
                                act.wait_ge(S["conv_done"], i - 1)
                            me.do(A(up[:, slot:slot + 2, PAD:PAD + SEQ], src[:, :, 0:SEQ], ACT.Copy))
                            me.do(A(up[:, slot:slot + 2, PAD + SEQ + PAD:UPW], src[:, :, SEQ:T], ACT.Copy), "unit_out")
                        elif what == "tail":
                            me.do(A(baT[:, :], src[0:8, 0, :], ACT.Copy), "unit_out")
                        else:
                            if what == "z":
                                act.wait_ge(S["conv_done"], 6)
                                dst = z[:, 2 * i:2 * i + 2, :]
                            else:
                                dst = dict(qb=bq, kb=bk, vb=bv, qc=bq, kc=bk, vc=bv, gc=gc)[what][:, :, :]
                            me.do(A(dst, src, ACT.Copy), "unit_out")
                    elif kind == "ba":
                        conv_silu()
                        act.wait_ge(S["gates_in"], 1)
                        me.do(A(gt[:, AX], gt[:, AX], ACT.Exp, scale=-1.0))
                        me.do(A(gt[:, BETA], bac[:, :, 0:H], ACT.Exp, scale=-1.0))
                        me.do(A(ea[:, :], ea[:, :], ACT.Exp))
                        me.do(A(gt[:, AX], gt[:, AX], ACT.Ln, bias=C("ones")[:, 0:1]), "gates_act")
                    elif kind == "ss":
                        for i in ((0, 1) if t == 0 else (t + 1,) if t < 7 else ()):
                            me.do(A(tmp[:, i, :], qkv[:, i, :], ACT.Square), "sq2_done")
                        wait_filled(act, step)
                        if t >= 2:
                            act.wait_ge(S["qk_normed"], t - 1)
                        me.drain(A(rn[:, t % 2, :], small(step)[:, 0:CW], ACT.Ln, bias=C("eps")), step)
                        if t < 4:
                            me.do(A(rn[:, t % 2, :], rn[:, t % 2, :], ACT.Exp, bias=C("qscale"), scale=-0.5), "rn_done")
                        else:
                            me.do(A(rn[:, t % 2, :], rn[:, t % 2, :], ACT.Exp, scale=-0.5), "rn_done")
                    elif kind == "dcol":
                        wait_drained(act, step)
                        me.do(A(gt[:, ED], gt[:, ND], ACT.Exp, scale=-1.0), "ed_done")
                    elif kind == "D":
                        if t:
                            wait_drained(act, ("Su", t - 1))
                        wait_filled(act, step)
                        me.do(A(eD[:, :, 0:L], wide(small(step)), ACT.Exp), "eD_done")
                        wait_drained(act, step)
                        me.do(A(lm[0:L, :, 0:L], lm[0:L, :, 0:L], ACT.Exp), "lm_done")
                    elif kind == "kt":
                        wait_filled(act, step)
                        for h in range(H):
                            ins = A(kt[0:L, h, :], small(step)[0:L, h * P:(h + 1) * P], ACT.Copy, scale=lm[0:L, h, L - 1:L])
                            me.drain(ins, step) if h == H - 1 else me.do(ins)
                    elif kind == "T1":
                        wait_filled(act, step)
                        me.drain(A(Vn[0:L, :, 0:L], wide(small(step))[0:L], ACT.Copy), step)
                    elif kind == "Y":
                        wait_filled(act, step)
                        me.drain(A(Ysb[0:L, :, 0:L], wide(small(step))[0:L], ACT.Copy), step)
                    elif kind == "vn":
                        wait_filled(act, step)
                        me.drain(A(vn[0:L, :, :].rearrange("p h v -> p (h v)"), small(step)[0:L, :], ACT.Copy), step)
                    elif kind == "o":
                        wait_filled(act, step)
                        me.do(A(qkv[:, 0:H, p0:p0 + L], wide(small(step)), ACT.Copy))
                        me.drain(A(osq[:, 0:H * L], small(step)[:, 0:H * L], ACT.Square), step)
                    elif kind in ("on", "cv"):
                        wait_filled(act, step)
                        i = NORMED.index(step)
                        if i:
                            act.wait_ge(S["gated"], i)
                        n, scale = (H * L, 1.0 / P) if kind == "on" else (T, 1.0)
                        rsqrt(rno[:, 0:n], small(step)[:, 0:n], scale, me, step, "gn_done")
                    elif kind == "btok":
                        wait_filled(act, step)
                        me.do(A(btk[0:L, t, :], small(step)[0:L, 0:256], ACT.Copy))
                        me.drain(A(btv[0:L, t, :], small(step)[0:L, 256:512], ACT.Copy), step)
                    elif kind == "bkc":
                        wait_filled(act, step)
                        me.drain(A(kcT[:, :, :].rearrange("p b t -> p (b t)"), small(step)[:, 0:256], ACT.Copy), step)
                    elif kind == "lc":
                        wait_filled(act, step)
                        me.drain(A(lastr[:, :], small(step)[0:2 * PAD * CB, 0:P], ACT.Copy), step)
                    elif kind == "sB":
                        act.wait_ge(S["maxima"], t + 1)
                        for n, (rows, a, b) in enumerate(((P, 0, P), (P, P, 3 * P), (DEC, 384, 576))):
                            me.do(A(prob[0:rows, a:b], prob[0:rows, a:b], ACT.Exp, bias=mx[0:rows, 0, n:n + 1],
                                    accum_out=mx[0:rows, 1, n:n + 1]), "exps" if n == 2 else None)
                    elif kind == "pT":
                        wait_filled(act, step)
                        me.do(A(pT[:, 0:448], small(step)[:, 0:448], ACT.Copy))
                        me.drain(A(pT[0:DEC, 448:512], small(step)[0:DEC, 448:512], ACT.Copy), step)
                    elif kind == "oB":
                        wait_filled(act, step)
                        r = slice(64 * (t % 2), 64 * (t % 2) + 64)
                        me.drain(A(tmp[r, 4 + t // 2, 0:T], small(step)[r, 0:T], ACT.Copy), step)
                    elif kind == "zs":
                        me.do(A(z[:, :, :], z[:, :, :], ACT.Silu), "z_done")
                    elif kind == "gs":
                        me.do(A(gc[:, :, :], gc[:, :, :], ACT.Silu), "gc_done")
                    elif kind == "oC":
                        wait_filled(act, step)
                        me.drain(A(oC[:, :, c0:c0 + L], small(step)[:, 0:256].rearrange("p (b l) -> p b l", b=2)[:, :, 0:L],
                                   ACT.Copy), step)
                    elif kind == "cm":
                        wait_drained(act, step)
                        me.do(A(rsc[:, :], oC[:, t, :], ACT.Square), "oc_sq")

                act.wait_ge(S["gated"], len(NORMED))
                for k in range(KD):
                    me.do(A(hh[:, k, :], tmp[:, k, 0:T], ACT.Copy), "hh_done")
                for d in range(4):
                    split_hi(layer, U_OUT + d + 1)
                    act.wait_ge(S["x_updated"], SQ_OUT + d + 1)
                    at = slice(2 * d, 2 * d + 2)
                    me.do_at(A(tmp[:, at, 0:T], xT[:, at, :], ACT.Square), S["sq_done"], SQ_OUT + d + 1)
                statistics(1, me)
                apply_norm(3, 2, me)
                act.wait_ge(stored, (layer + 1) * 16 * STORES)
                ffn(layer, U_FFN2, 1, 3, me)
                statistics(2, me)

            for t, (_, _, L) in enumerate(TILES):
                for half in range(2):
                    act.wait_ge(S["y_turned"], 2 * t + half + 1)
                    me.do(A(tok[0:L, t, half * 512:half * 512 + 512], psum[0:L, 2 * t + half, :], ACT.Copy), "y_out")

        @block.vector
        def _(dve):
            V = dve

            def split_lo(layer, u, i=0, width=SLOT):
                dve.wait_ge(hi_done, layer * UNITS + 4 * i + u + 1)
                s = u % SPLIT
                V.tensor_tensor(wlo[:, s, 0:width], raw[:, u % RAW, 0:width], whi[:, s, 0:width].bitcast(F32),
                                ALU.subtract).then_inc(lo_done, 1)
                dve.wait_ge(lo_done, layer * UNITS + 4 * i + u + 1 + RAW)

            def wait_products(layer, u, i=0):
                dve.wait_ge(unit_used, layer * UNITS + 4 * i + u + 1 + SPLIT)

            def low_parts(k, me):
                dve.wait_ge(S["hh_done"], me.counts.get("hl_done", 0) + 1)
                me.do(V.tensor_tensor(hl[:, k, :], tmp[:, k, 0:T], hh[:, k, :].bitcast(F32), ALU.subtract), "hl_done")

            def apply_norm(col, me):
                for k in range(KD):
                    me.do(V.scalar_tensor_tensor(tmp[:, k, 0:T], xT[:, k, :], par[:, col + k:col + k + 1], rstd[:, :],
                                                 ALU.mult, ALU.mult), "hf_done")
                    if k:
                        low_parts(k - 1, me)
                low_parts(KD - 1, me)

            def ffn(layer, u0, f, me):
                def gate_up(n, i):
                    u = u0 + 2 * n
                    at = bass.ds(2 * (2 * i + n), 2)
                    split_lo(layer, u + 1, i)
                    split_lo(layer, u + 2, i)
                    wait_products(layer, u + 1, i)
                    dve.wait_ge(S["gate_silu"], NJ * f + 2 * i + n + 1)
                    if n:
                        dve.wait_ge(S["act_hi_done"], NJ * f + 2 * i + n)
                    me.do_at(V.tensor_tensor(prod[:, :, :], gs[:, :, :], psum[:, 2:4, 0:T], ALU.mult), S["product"],
                              NJ * f + 2 * i + n + 1)
                    dve.wait_ge(S["act_hi_done"], NJ * f + 2 * i + n + 1)
                    me.do_at(V.tensor_tensor(act_lo[:, at, :], prod[:, :, :], act_hi[:, at, :].bitcast(F32),
                                              ALU.subtract), S["act_lo_done"], NJ * f + 2 * i + n + 1)

                def down(n, i):
                    u = u0 + 2 * NJ + 2 * n
                    for r in range(2):
                        if u + r + 1 < UNITS:
                            split_lo(layer, u + r + 1, i, SLOT if n == KD - 1 and r else DOWN_K * P)
                    wait_products(layer, u + 1, i)
                    x = xT[:, bass.ds(2 * i + n, 1), :].rearrange("p a t -> p (a t)")
                    me.do_at(V.scalar_tensor_tensor(x, psum[:, n % 2, 0:T], 0.5, x, ALU.mult, ALU.add), S["x_updated"],
                              SQ0[f] + 2 * i + n + 1)

                in_turn(dve, 1, NJ, 0, gate_up)
                in_turn(dve, 2, KD, 2, down)

            dve.drain().then_inc(arrived, 1)
            with dve.Fori(0, DEPTH) as layer:
                dve.wait_ge(layer_open, layer + 1)
                me = Engine(dve, "dve_step")
                split_lo(layer, 0)
                wait_filled(dve, ("par",))
                me.drain(V.tensor_copy(par[:, :], small(("par",))[:, 0:NPAR]), ("par",))
                apply_norm(R_F1, me)
                ffn(layer, U_FFN1, 0, me)
                dve.wait_ge(S["rstd_done"], 1)
                apply_norm(R_MIX, me)

                me.do(V.memset(up[:, :, 0:PAD], 0.0))
                me.do(V.memset(bac[:, :, :], 0.0))
                me.do(V.memset(gt[:, ND], 0.0))
                me.do(V.memset(mx[:, :, :], 1.0))
                for step in STEPS:
                    kind, t = step[0], (step[1] if len(step) > 1 else None)
                    bank = small(step) if step in USE else None
                    if kind not in ("unit", "zs", "gs", "ba", "ss", "dcol", "bkc", "lc", "sA", "sB", "pT", "oB", "rot",
                                    "cm", "cv"):
                        c0, p0, L = TILES[t]
                        wide = lambda x: x[:, 0:H * L].rearrange("p (h l) -> p h l", h=H)
                        mask = lambda name: C(name, L, L)[:, None, :].to_broadcast([L, H, L])
                    if kind == "unit":
                        if t < 15:
                            split_lo(layer, U_IN + t + 1, 0, KD * P if IN_UNITS[t + 1][0] == "tail" else SLOT)
                        else:
                            split_lo(layer, U_OUT)
                        what, i, _ = IN_UNITS[t]
                        if what == "conv":
                            dve.wait_ge(S["unit_out"], t + 1)
                            slot = 2 * (i % 2)
                            state = par[:, R_STATE:R_STATE + PAD * CB].rearrange("p (r b) -> p b r", r=PAD)
                            me.do(V.tensor_copy(up[:, slot:slot + 2, PAD + SEQ:PAD + SEQ + PAD],
                                                state[:, 2 * i:2 * i + 2, :]))
                            for s, end in enumerate((PAD + SEQ, UPW)):
                                me.do(V.tensor_copy(lastc[:, s, :, 2 * i:2 * i + 2].rearrange("p r b -> p b r"),
                                                    up[:, slot:slot + 2, end - PAD:end]))
                            for c in range(2):
                                b = 2 * i + c
                                w = lambda j: par[:, R_CONV + j * CB + b:R_CONV + j * CB + b + 1]
                                me.do(V.tensor_scalar(qkv[:, b, :], up[:, slot + c, 0:CW], w(0), None, ALU.mult))
                                for j in range(1, CONV_W):
                                    me.do(V.scalar_tensor_tensor(qkv[:, b, :], up[:, slot + c, j:j + CW], w(j),
                                                                 qkv[:, b, :], ALU.mult, ALU.add),
                                          "conv_done" if c and j == CONV_W - 1 else None)
                    elif kind == "ba":
                        wait_filled(dve, step)
                        me.do(V.tensor_copy(bac[:, 0:2, :].rearrange("p t c -> p (t c)"), bank[:, 0:16]))
                        me.drain(V.tensor_copy(bac[0:DEC, 2, :], bank[0:DEC, 16:24]), step)
                        dve.wait_ge(gate_loaded, (layer + 1) * 32)
                        per_tile = lambda x: x[:, None, :].to_broadcast([P, 3, H])
                        me.do(V.tensor_tensor(gt[:, GX], bac[:, :, H:2 * H], per_tile(dtb), ALU.add))
                        me.do(V.tensor_scalar(gt[:, RX], gt[:, GX], 0.0, None, ALU.max))
                        me.do(V.tensor_scalar(gt[:, AX], gt[:, GX], -1.0, None, ALU.mult))
                        me.do(V.tensor_tensor(gt[:, AX], gt[:, AX], gt[:, GX], ALU.max), "gates_in")
                        dve.wait_ge(S["gates_act"], 1)
                        me.do(V.tensor_tensor(gt[:, AX], gt[:, AX], gt[:, RX], ALU.add))
                        me.do(V.scalar_tensor_tensor(gt[:, G], gt[:, AX], -1.0, per_tile(ea), ALU.mult, ALU.mult))
                        me.do(V.tensor_scalar(gt[:, BETA], gt[:, BETA], 1.0, None, ALU.add))
                        me.do(V.reciprocal(gt[:, BETA], gt[:, BETA]), "gates_done")
                    elif kind == "ss":
                        dve.wait_ge(S["rn_done"], t + 1)
                        me.do(V.tensor_tensor(qkv[:, t, :], qkv[:, t, :], rn[:, t % 2, :], ALU.mult), "qk_normed")
                    elif kind == "dcol":
                        wait_filled(dve, step)
                        me.do(V.tensor_scalar(gt[:, ND, 0:2], bank[:, 0:8].rearrange("p (t h) -> p t h", h=H), -1.0, None,
                                              ALU.mult))
                        me.drain(V.tensor_scalar(gt[0:DEC, ND, 2], bank[0:DEC, 8:12], -1.0, None, ALU.mult), step)
                        dve.wait_ge(S["ed_done"], 1)
                        me.do(V.scalar_tensor_tensor(gt[:, NBE], gt[:, BETA], -1.0, gt[:, ED], ALU.mult, ALU.mult))
                    elif kind == "vt":
                        wait_filled(dve, step)
                        for h in range(H):
                            ins = V.tensor_scalar(vb[0:L, h, :], bank[0:L, h * P:(h + 1) * P], gt[0:L, BETA, t, h:h + 1],
                                                  None, ALU.mult)
                            me.drain(ins, step) if h == H - 1 else me.do(ins)
                    elif kind == "D":
                        dve.wait_ge(S["eD_done"], t + 1)
                        wait_filled(dve, step)
                        for h in range(H):
                            ins = V.scalar_tensor_tensor(lm[0:L, h, 0:L], bank[0:L, h * L:(h + 1) * L],
                                                         gt[0:L, ND, t, h:h + 1], C("future", L, L), ALU.add, ALU.add)
                            me.drain(ins, step) if h == H - 1 else me.do(ins)
                    elif kind == "G":
                        dve.wait_ge(S["lm_done"], t + 1)
                        wait_filled(dve, step)
                        me.drain(V.tensor_tensor(U[0:L, :, 0:L], wide(bank)[0:L], lm[0:L, :, 0:L], ALU.mult), step)
                        wait_filled(dve, ("Bb", t))
                        me.drain(V.tensor_tensor(U[0:L, :, 0:L], wide(small(("Bb", t)))[0:L], U[0:L, :, 0:L], ALU.mult),
                                 ("Bb", t))
                    elif kind == "QK":
                        wait_filled(dve, step)
                        me.drain(V.tensor_tensor(aT[0:L, :, 0:L], wide(bank)[0:L], lm[0:L, :, 0:L], ALU.mult), step)
                        if t:
                            q = qkv[:, 0:H, p0:p0 + L]
                            me.do(V.tensor_tensor(q, q, eD[:, :, 0:L], ALU.mult), "qs_done")
                        me.do(V.tensor_tensor(Vt[0:L, :, 0:L], U[0:L, :, 0:L], mask("level1"), ALU.mult))
                        me.do(V.tensor_tensor(Vt[0:L, :, 0:L], mask("ident"), Vt[0:L, :, 0:L], ALU.subtract))
                        me.do(V.tensor_tensor(Us[0:L, :, 0:L], U[0:L, :, 0:L], mask("level2"), ALU.mult), "tri_done")
                    elif kind == "Z":
                        s = step[2]
                        wait_filled(dve, ("Zt", t, s))
                        if s != LEVELS[t][-1]:
                            wait_filled(dve, step)
                        me.drain(V.tensor_tensor(Vt[0:L, :, 0:L], Vt[0:L, :, 0:L], wide(small(("Zt", t, s)))[0:L],
                                                 ALU.subtract), ("Zt", t, s))
                        if s != LEVELS[t][-1]:
                            me.drain(V.tensor_tensor(Vn[0:L, :, 0:L], Vn[0:L, :, 0:L], wide(bank)[0:L], ALU.subtract), step)
                            me.do(V.tensor_tensor(Us[0:L, :, 0:L], U[0:L, :, 0:L], mask(f"level{2 * s}"), ALU.mult),
                                  "level_done")
                    elif kind == "kS":
                        wait_filled(dve, step)
                        for h in range(H):
                            ins = V.scalar_tensor_tensor(vb[0:L, h, :], bank[0:L, h * P:(h + 1) * P],
                                                         gt[0:L, NBE, t, h:h + 1], vb[0:L, h, :], ALU.mult, ALU.add)
                            me.drain(ins, step) if h == H - 1 else me.do(ins)
                    elif kind == "Su":
                        wait_filled(dve, step)
                        state = pS if t < 2 else sS
                        if t == 0:
                            me.drain(V.tensor_copy(state[:, :, :].rearrange("p h v -> p (h v)"), bank[:, :]), step)
                        else:
                            for h in range(H):
                                ins = V.scalar_tensor_tensor(state[:, h, :], state[:, h, :], eD[:, h, L - 1:L],
                                                             bank[:, h * P:(h + 1) * P], ALU.mult, ALU.add)
                                me.drain(ins, step) if h == H - 1 else me.do(ins)
                    elif kind == "on":
                        dve.wait_ge(S["gn_done"], NORMED.index(step) + 1)
                        dve.wait_ge(S["z_done"], 1)
                        dst = tmp[:, 0:H, c0:c0 + L]
                        me.do(V.tensor_tensor(dst, qkv[:, 0:H, p0:p0 + L], wide(rno), ALU.mult))
                        me.do(V.scalar_tensor_tensor(dst, dst, par[:, R_GDN:R_GDN + 1], z[:, :, c0:c0 + L], ALU.mult,
                                                     ALU.mult), "gated")
                    elif kind == "sA":
                        if t:
                            wait_filled(dve, ("pT", t - 1))
                        dve.wait_ge(S["bias_masked"], 1)
                        wait_filled(dve, step)
                        me.do(V.scalar_tensor_tensor(prob[:, 0:P], bank[:, 0:P], 0.125, bias[:, t, P:2 * P], ALU.mult,
                                                     ALU.add))
                        me.drain(V.scalar_tensor_tensor(prob[:, P:384], bank[:, P:384], 0.125, bias[:, t, :], ALU.mult,
                                                        ALU.add), step)
                    elif kind == "sB":
                        wait_filled(dve, step)
                        me.drain(V.scalar_tensor_tensor(prob[0:DEC, 384:576], bank[0:DEC, 0:192], 0.125,
                                                        bias[0:DEC, t, 0:192], ALU.mult, ALU.add), step)
                        parts = ((P, 0, P), (P, P, 384), (DEC, 384, 576))
                        for n, (rows, a, b) in enumerate(parts):
                            me.do(V.tensor_reduce(mx[0:rows, 0, n:n + 1], prob[0:rows, a:b], AX_X, ALU.max))
                        me.do(V.tensor_scalar(mx[:, 0, :], mx[:, 0, :], -1.0, None, ALU.mult), "maxima")
                        dve.wait_ge(S["exps"], t + 1)
                        me.do(V.reciprocal(mx[:, 2, :], mx[:, 1, :]))
                        for n, (rows, a, b) in enumerate(parts):
                            me.do(V.tensor_scalar(prob[0:rows, a:b], prob[0:rows, a:b], mx[0:rows, 2, n:n + 1], None,
                                                  ALU.mult), "probs" if n == 2 else None)
                    elif kind == "rot":
                        x = (bq, bk)[t // 2][:, t % 2, :]
                        wait_filled(dve, step)
                        me.drain(V.tensor_tensor(rsc[:, :], bank[:, 0:T], C("sin"), ALU.mult), step)
                        me.do(V.tensor_tensor(x, x, C("cos"), ALU.mult))
                        me.do(V.tensor_tensor(x, x, rsc[:, :], ALU.add), "rope_done")
                    elif kind == "ctok":
                        wait_filled(dve, step)
                        gk = C(f"gk{L}", L)[:, :, None].to_broadcast([L, H, 64])
                        me.do(V.tensor_tensor(ctk[0:L, :].rearrange("p (h d) -> p h d", h=H),
                                              bank[0:L, 0:256].rearrange("p (h d) -> p h d", h=H), gk, ALU.mult))
                        me.drain(V.tensor_copy(ctv[0:L, :], bank[0:L, 256:512]), step)
                    elif kind == "cqk":
                        wait_filled(dve, step)
                        at, _ = CAT["dmask0"]
                        decay = cst[:, at:at + H * P].rearrange("p (h l) -> p h l", h=H)
                        if L < P:
                            me.do(V.memset(aC[L:P, :, 0:L], 0.0))
                        me.drain(V.tensor_tensor(aC[0:L, :, 0:L], wide(bank)[0:L], decay[0:L, :, 0:L], ALU.mult), step)
                        if t:
                            at, _ = CAT["gq0"]
                            gq = cst[:, at:at + 2 * P].rearrange("p (b l) -> p b l", b=2)
                            me.do(V.tensor_tensor(bq[:, :, c0:c0 + L], bq[:, :, c0:c0 + L], gq[:, :, 0:L], ALU.mult),
                                  "qd_done")
                    elif kind == "R":
                        wait_filled(dve, step)
                        rstate = pR if t < 2 else sR
                        if t == 0:
                            me.drain(V.tensor_copy(rstate[:, :, :].rearrange("p b v -> p (b v)"), bank[:, 0:P]), step)
                        else:
                            for b in range(2):
                                ins = V.scalar_tensor_tensor(rstate[:, b, :], rstate[:, b, :], C(f"gl{L}")[:, b:b + 1],
                                                             bank[:, b * 64:b * 64 + 64], ALU.mult, ALU.add)
                                me.drain(ins, step) if b else me.do(ins)
                    elif kind == "cm":
                        wait_filled(dve, step)
                        me.drain(V.tensor_tensor(oC[:, t, :], oC[:, t, :], bank[:, 0:T], ALU.subtract), step)
                    elif kind == "cv":
                        dve.wait_ge(S["gn_done"], NORMED.index(step) + 1)
                        dve.wait_ge(S["gc_done"], 1)
                        dst = tmp[:, 6 + t, 0:T]
                        me.do(V.tensor_tensor(dst, oC[:, t, :], rno[:, 0:T], ALU.mult))
                        me.do(V.tensor_tensor(dst, dst, gc[:, t, :], ALU.mult), "gated")

                for k in range(KD):
                    low_parts(k, me)
                for d in range(4):
                    split_lo(layer, U_OUT + d + 1)
                    wait_products(layer, U_OUT + d)
                    x = xT[:, 2 * d:2 * d + 2, :]
                    me.do_at(V.tensor_tensor(x, psum[:, 2 * (d % 2):2 * (d % 2) + 2, 0:T], x, ALU.add), S["x_updated"],
                              SQ_OUT + d + 1)
                dve.wait_ge(S["rstd_done"], 2)
                apply_norm(R_F2, me)
                ffn(layer, U_FFN2, 1, me)
                dve.drain().then_inc(arrived, 1)

            dve.wait_ge(S["rstd_done"], 3)
            for k in range(KD):
                me.do(V.scalar_tensor_tensor(tmp[:, k, 0:T], xT[:, k, :], par[:, R_FINAL + k:R_FINAL + k + 1],
                                             rstd[:, :], ALU.mult, ALU.mult), "y_normed")


_INS = ["x_prompt", "x_sample", "state_gdn", "state_conv", "cache_band_k", "cache_band_v", "state_ret", "norm_ffn1",
        "w_ffn1_gate", "w_ffn1_up", "w_ffn1_down", "norm_mix", "w_in", "conv_w", "a_log", "dt_bias", "gdn_norm",
        "rel_bias", "w_out", "norm_ffn2", "w_ffn2_gate", "w_ffn2_up", "w_ffn2_down", "norm_final"]
_OUTS = [(1, SEQ, D_MODEL), (1, DEC, D_MODEL),
         (DEPTH, 1, H, 128, 128), (DEPTH, 1, PAD, CONV_DIM), (DEPTH, 1, SEQ, H, 64), (DEPTH, 1, SEQ, H, 64),
         (DEPTH, 1, H, 64, 64),
         (DEPTH, 1, H, 128, 128), (DEPTH, 1, PAD, CONV_DIM), (DEPTH, 1, DEC, H, 64), (DEPTH, 1, DEC, H, 64),
         (DEPTH, 1, H, 64, 64)]


def kernel(**inputs):
    import concourse.bacc as bacc
    from concourse.bass_utils import run_bass_kernel_spmd

    nc = bacc.Bacc("TRN2", target_bir_lowering=False, num_devices=1)
    arrays, args = {}, []
    for name in _INS:
        arrays[f"in_{name}"] = np.ascontiguousarray(inputs[name])
    arrays["in_consts"] = constants()[0]
    for name, a in arrays.items():
        args.append(nc.dram_tensor(name, a.shape, mybir.dt.from_np(a.dtype), kind="ExternalInput").ap())
    for i, shape in enumerate(_OUTS):
        args.append(nc.dram_tensor(f"out_{i}", shape, F32, kind="ExternalOutput").ap())
    build(nc, *args)
    r = run_bass_kernel_spmd(nc, [arrays], core_ids=[0])
    return tuple(r.results[0][f"out_{i}"] for i in range(len(_OUTS)))
```

```python
from contextlib import ExitStack
import math

import numpy as np

import concourse.bass as bass
from concourse import mybir

F32 = mybir.dt.float32
F32R = mybir.dt.float32r
ACT = mybir.ActivationFunctionType
ALU = mybir.AluOpType
AX_X = mybir.AxisListType.X

P = 128
DEPTH, D_MODEL, D_FF = 2, 1024, 2816
SEQ, DEC = 256, 64
T = SEQ + DEC
PAST = 128
EPS = 1e-6
NEG = -1e30
KD = D_MODEL // P
KF = D_FF // P
NJ = KF // 2
H = 4
CONV_W, CONV_DIM = 4, 1536
CB = CONV_DIM // P
TAIL0 = 2048
PAD = CONV_W - 1
UPW = PAD + SEQ + PAD + DEC
CW = UPW - PAD
TILES = [(0, 0, 128), (128, 128, 128), (256, 256 + PAD, 64)]

LN_EXP = "natural_log_exp_and_others"

RAW, SPLIT = 4, 2
SLOT = 2048
DOWN_K = KF // 2
U_FFN = 2 * NJ + 2 * KD
U_FFN1, U_IN, U_OUT, U_FFN2 = 0, U_FFN, U_FFN + 16, U_FFN + 20
UNITS = 2 * U_FFN + 20
assert UNITS % RAW == 0

R_F1, R_MIX, R_F2, R_CONV, R_GDN, R_STATE, R_FINAL = 0, 8, 16, 24, 72, 73, 109
NPAR = 117
BUFFERS = ("vb", "kt", "aT", "Vt", "U", "Us", "Vn", "Ysb", "lm")
PAR_LOADS = 8

FIRST_CONSTS = 2 * P + 2

IN_UNITS = ([("conv", i, 256 * i) for i in range(4)] + [("tail", 0, TAIL0)]
            + [("conv", i, 256 * i) for i in (4, 5)]
            + [("kb", 0, 2312), ("qb", 0, 2056), ("vb", 0, 2568), ("z", 0, 1536), ("z", 1, 1792),
               ("qc", 0, 2824), ("kc", 0, 3080), ("vc", 0, 3336), ("gc", 0, 3592)])
CONV_UNIT = [0, 1, 2, 3, 5, 6]

LEVELS = {t: [s for s in (2, 4, 8, 16, 32, 64) if s < L] for t, (_, _, L) in enumerate(TILES)}


def weave(a, b):
    out, done = [], 0
    for i, x in enumerate(a):
        out.append(x)
        while done < len(b) and done * len(a) < (i + 1) * len(b):
            out.append(b[done])
            done += 1
    return out + b[done:]


def unit_steps(*ns):
    steps = []
    for n in ns:
        steps += [("part", n, i) for i in range(2 if IN_UNITS[n][0] == "tail" else 4)]
        if n < 15:
            steps += [("hi", n + 2), ("lo", n + 2)]
        steps += [("out", n)]
    return steps


def mix_steps():
    def levels(t):
        return [[("Y", t, s), ("Z", t, s)] for s in LEVELS[t]]

    steps, pairs, squares = [("hi", 1), ("lo", 1)], 0, 0
    for n in range(7):
        steps += unit_steps(n)
        if pairs and n in CONV_UNIT:
            steps += [("silu", pairs - 1)]
        if squares < 8 and ("silu", squares // 2) in steps:
            steps += [("sq", squares), ("sq", squares + 1)]
            squares += 2
        if n in CONV_UNIT:
            steps += [("conv", pairs)]
            pairs += 1
    steps += [("ba",)] + unit_steps(7) + [("silu", pairs - 1)]
    steps += weave([("exps",), ("ss", 0), ("ss", 1), ("gates",), ("ss", 2), ("ss", 3), ("dcol",), ("vt", 0), ("vt", 1)]
                   + [("ss", 4), ("ss", 5), ("D", 0), ("ss", 6), ("ss", 7), ("D", 1), ("Bb", 0), ("G", 0), ("Bb", 1),
                      ("G", 1)], unit_steps(8, 9, 10))
    chain = [(kind, t) for kind in ("QK", "kt", "T1") for t in range(2)]
    for a, b in zip(levels(0), levels(1)):
        chain += [a[0], b[0], a[1], b[1]]
    z_unit, heads = unit_steps(11), []
    for h in range(H):
        heads += [("sA", h), ("sB", h)] + z_unit[:2] + [("pT", h), ("oB", h)]
        z_unit = z_unit[2:]
    heads.insert(-2, ("zs",))
    steps += weave(chain, [("btok", 0), ("btok", 1), ("btok", 2), ("bkc",)] + heads + [("lc",)])
    state_chain = [(kind, t) for t in range(2) for kind in ("kS", "vn", "o", "Su", "on") if (kind, t) != ("kS", 0)]
    inverse = [(kind, 2) for kind in ("vt", "D", "Bb", "G", "QK", "kt", "T1")] + [s for pair in levels(2) for s in pair]
    retention = [(kind, t) for t in range(3) for kind in ("ctok", "cqk", "oC", "R")]
    last = [(kind, 2) for kind in ("kS", "vn", "o", "on", "Su")]
    steps += weave(weave(inverse, state_chain) + last,
                   unit_steps(12, 13) + [("rot", 0), ("rot", 1)] + unit_steps(14) + [("rot", 2), ("rot", 3)]
                   + retention[:4] + weave(retention[4:], unit_steps(15) + [("gs",)])
                   + [("cm", 0), ("cm", 1), ("cv", 0), ("cv", 1)]
                   + [("split", 0), ("split", 1), ("project", 0), ("project", 1)])
    steps += [("split", i) for i in range(2, KD)] + [("project", i) for i in range(2, KD)]
    return steps


STEPS = mix_steps()
SPLIT_ORDER = (4, 5, 0, 1, 2, 3, 6, 7)
NO_BANK = ("hi", "lo", "part", "out", "conv", "silu", "sq", "exps", "gates", "zs", "gs", "split",
           "project")
PER_TILE = ("vt", "D", "Bb", "G", "QK", "kt", "T1", "Y", "Z", "kS", "vn", "o", "Su", "on", "btok", "ctok", "cqk", "oC",
            "R")


def small_uses():
    yield ("stat", 0)
    for s in STEPS:
        if s[0] == "Z":
            yield ("Zt",) + s[1:]
            if s[2] != LEVELS[s[1]][-1]:
                yield s
        elif s[0] not in NO_BANK:
            yield s
    yield ("stat", 1)
    yield ("stat", 2)


NORMED = [s for s in STEPS if s[0] in ("on", "cv")]
LEVEL_DONE = {s[1:]: i + 1 for i, s in enumerate(s for s in STEPS if s[0] == "Z" and s[2] != LEVELS[s[1]][-1])}
assert STEPS.index(("bkc",)) < min(STEPS.index(("kS", 2)), STEPS.index(("oC", 2)))
assert STEPS.index(("oB", H - 1)) < STEPS.index(("out", 12))
SQ0, SQ_OUT = (0, 12), 8
ADD0, ADD_OUT = (0, KD), KD - 2
STORES = 10

USE = {key: (i % 4, i // 4) for i, key in enumerate(small_uses())}


def constants():
    i = np.arange(P)
    f = np.float32
    parts = {}
    parts["ident"] = np.eye(P, dtype=f)
    parts["ones"] = np.ones((P, P), f)
    parts["eps"] = np.full((P, 1), EPS, f)
    parts["qscale"] = np.full((P, 1), -0.5 * math.log(128.0), f)
    parts["utri"] = (i[:, None] <= i[None, :]).astype(f)
    parts["future"] = np.where(i[:, None] <= i[None, :], 0, NEG).astype(f)
    for s in (1, 2, 4, 8, 16, 32, 64):
        j, q = i[:, None], i[None, :]
        parts[f"level{s}"] = ((j // (2 * s) == q // (2 * s)) & (j // s % 2 == 0) & (q // s % 2 == 1)).astype(f)
    rot = np.zeros((P, P), f)
    for m in range(P):
        if m % 64 < 32:
            rot[m + 32, m] = -1.0
        else:
            rot[m - 32, m] = 1.0
    parts["rot"] = rot
    parts["mean64"] = (i[:, None] // 64 == i[None, :] // 64).astype(f) / f(64)
    half = 32
    inv_freq = np.exp(f(-math.log(10000.0)) * np.arange(half, dtype=f) / f(half)).astype(f)
    pos = np.concatenate([np.arange(SEQ), PAST + np.arange(DEC)]).astype(f)
    ang = (inv_freq[i % 32][:, None] * pos[None, :]).astype(f)
    parts["cos"] = np.cos(ang).astype(f)
    parts["sin"] = np.sin(ang).astype(f)
    lg = np.log1p(-np.exp2(-5.0 - np.arange(H)))
    d = (i[None, :] - i[:, None])
    for h in range(H):
        parts[f"dmask{h}"] = np.where(d >= 0, np.exp(lg[h] * np.maximum(d, 0)) * 0.125, 0).astype(f)
    for b in range(2):
        parts[f"gq{b}"] = np.exp(lg[2 * b + i // 64][:, None] * (i[None, :] + 1.0)).astype(f)
    for L in (128, 64):
        parts[f"gk{L}"] = (np.exp(lg[None, :] * (L - 1.0 - i[:, None])) * 0.125).astype(f)
        parts[f"gl{L}"] = np.stack([np.exp(lg[2 * b + i // 64] * L) for b in range(2)], 1).astype(f)
    at, n = {}, 0
    for k, v in parts.items():
        at[k] = (n, v.shape[1])
        n += v.shape[1]
    return np.concatenate(list(parts.values()), 1), at


def build(nc, x_prompt, x_sample, state_gdn, state_conv, cache_k, cache_v, state_ret, norm_ffn1, w_g1, w_u1, w_d1,
          norm_mix, w_in, conv_w, a_log, dt_bias, gdn_norm, rel_bias, w_out, norm_ffn2, w_g2, w_u2, w_d2,
          norm_final, consts, y_prompt, y_sample, p_gdn, p_conv, p_k, p_v, p_ret, s_gdn, s_conv, s_k, s_v, s_ret):
    _, CAT = constants()
    ctx = ExitStack()
    with ctx:
        def sb(name, shape, dt=F32):
            return ctx.enter_context(nc.sbuf_tensor(name, shape, dt))

        def sem(name):
            return ctx.enter_context(nc.semaphore(name))

        bias_copies = nc.dram_tensor("bias_copies", (P, H, 384), F32, kind="Internal")

        cst = sb("cst", [P, consts.shape[1]])
        xT = sb("xT", [P, KD, T])
        hh = sb("hh", [P, KD, T], F32R)
        hl = sb("hl", [P, KD, T], F32R)
        raw = sb("raw", [P, RAW, SLOT])
        whi = sb("whi", [P, SPLIT, SLOT], F32R)
        wlo = sb("wlo", [P, SPLIT, SLOT], F32R)
        tmp = sb("tmp", [P, 8, CW])
        rstd = sb("rstd", [P, T])
        par_all = sb("par_all", [P, DEPTH, NPAR])
        par = sb("par", [P, NPAR])
        bias = sb("bias", [P, H, 256])
        ck = sb("ck", [P, 256])
        cv = sb("cv", [P, 256])
        sS = sb("sS", [P, H, P])
        sR = sb("sR", [P, 2, 64])
        ea = sb("ea", [P, H])
        dtb = sb("dtb", [P, H])
        spare = sb("spare", [P, 6])

        with ExitStack() as ffn:
            act_hi = ffn.enter_context(nc.sbuf_tensor("act_hi", [P, KF, T], F32R))
            act_lo = ffn.enter_context(nc.sbuf_tensor("act_lo", [P, KF, T], F32R))
            gs = ffn.enter_context(nc.sbuf_tensor("gs", [P, 2, T], F32))
            prod = ffn.enter_context(nc.sbuf_tensor("prod", [P, 2, T], F32))
        with ExitStack() as ends:
            tok = ends.enter_context(nc.sbuf_tensor("tok", [P, 3, D_MODEL], F32))
            parrow = ends.enter_context(nc.sbuf_tensor("parrow", [NPAR, DEPTH, P], F32))
        with ExitStack() as shared:
            up = shared.enter_context(nc.sbuf_tensor("up", [P, 4, UPW], F32))
        with ExitStack() as shared:
            z = shared.enter_context(nc.sbuf_tensor("z", [P, 4, T], F32))
        sb("up_rest", [P, 4 * UPW])
        qkv = sb("qkv", [P, CB, CW])
        bq = sb("bq", [P, 2, T])
        bk = sb("bk", [P, 2, T])
        bv = sb("bv", [P, 2, T])
        gc = sb("gc", [P, 2, T])
        lastc = sb("lastc", [P, 2, PAD, CB])
        lastr = sb("lastr", [2 * PAD * CB, P])
        bac = sb("bac", [P, 3, 8])
        gt = sb("gt", [P, 8, 3, H])
        GX, AX, RX, G, BETA, ND, ED, NBE = range(8)
        rn = sb("rn", [P, 2, CW])
        edl = sb("edl", [P, 3, H])

        def square(buf, at=0, n=P):
            return buf.rearrange("p h l -> p (h l)")[:, at:at + H * n].rearrange("p (h l) -> p h l", h=H)

        B = []
        for t in range(2):
            names = "vb kt aT Vt U Us Vn" + (" Ysb lm" if t else "")
            B.append({n: sb(f"{n}{t}", [P, H, P])[:, :, :] for n in names.split()})
        B[0]["lm"], B[0]["Ysb"] = square(tmp[:, 0:4, :]), square(tmp[:, 0:4, :], H * P)
        half = H * DEC
        B.append(dict(U=square(B[1]["U"], 0, DEC), Us=square(B[1]["U"], half, DEC), Vn=square(B[1]["Us"], 0, DEC),
                      Ysb=square(B[1]["Us"], half, DEC), lm=square(B[1]["lm"], 0, DEC),
                      aT=square(B[1]["lm"], half, DEC), vb=B[1]["Vn"], kt=B[1]["Ysb"], Vt=square(rn[:, :, :], 0, DEC)))
        eD = square(tmp[:, 6:8, :])
        vn = B[0]["U"]
        osq, rno = (B[0][n].rearrange("p h l -> p (h l)") for n in ("Us", "Vn"))
        pS = sb("pS", [P, H, P])
        pR = sb("pR", [P, 2, 64])
        prob = sb("prob", [P, 2 * T])
        mx = sb("mx", [P, 3, 3])
        pT = sb("pT", [P, 512])
        btk = sb("btk", [P, 3, 256])
        btv = sb("btv", [P, 3, 256])
        kcT = ck[:, :].rearrange("p (b t) -> p b t", b=2)
        ctk, ctv = ck, cv
        aC = pT[:, :].rearrange("p (h l) -> p h l", h=H)
        oC = prob[:, :].rearrange("p (b l) -> p b l", b=2)
        rsc = sb("rsc", [P, T])
        baT = rsc[0:8, :]

        psum = ctx.enter_context(nc.psum_tensor("psum", [P, 8, 512], F32))

        def C(name, rows=P, cols=None):
            at, n = CAT[name]
            return cst[0:rows, at:at + (cols or n)]

        landed = [sem(f"landed{i}") for i in range(RAW)]
        hi_done = sem("hi_done")
        lo_done = sem("lo_done")
        unit_used = sem("unit_used")
        par_loaded = sem("par_loaded")
        par_turned = sem("par_turned")
        gate_loaded = sem("gate_loaded")
        state_loaded = sem("state_loaded")
        cache_loaded = sem("cache_loaded")
        row_loaded = sem("row_loaded")
        copies_stored = sem("copies_stored")
        bias_loaded = sem("bias_loaded")
        stored = sem("stored")
        layer_open = sem("layer_open")
        arrived = sem("arrived")
        signals = dict(
            gate_silu="ScalarE: silu of a gate step",
            product="VectorE: silu(gate) * up of a step",
            act_hi_done="ScalarE: its high parts",
            act_lo_done="VectorE: its low parts",
            x_updated="VectorE: a block (or pair) of x has its sum",
            sq_done="ScalarE: its squares",
            squares_added="GpSimd: those squares added to the first block's",
            rstd_done="ScalarE: 1 / rms of x",
            hf_done="VectorE: a block normed, float32",
            hh_done="ScalarE: its high part",
            hl_done="GpSimd: its low part",
            unit_out="ScalarE: a w_in unit's result in SBUF",
            conv_done="VectorE: a pair convolved",
            last_kept="GpSimd: a pair's last columns copied",
            pads_zero="VectorE: the prompt's pads are zero",
            silu_done="ScalarE: silu of a convolved pair",
            sq2_done="ScalarE: squares of a head's q or k",
            rn_done="ScalarE: its 1 / norm",
            qk_normed="VectorE: q or k of a head normed",
            gates_in="VectorE: a + dt_bias split for softplus",
            gates_act="ScalarE: the gates' exponentials",
            gates_done="VectorE: g and beta of every token",
            spread="GpSimd: a tile's gates spread over the columns",
            ed_done="ScalarE: exp(decay) by token",
            eD_done="ScalarE: exp(decay) along the columns",
            lm_done="ScalarE: the decay's mask",
            tri_done="VectorE: inverse of the blocks of two",
            level_done="VectorE: the next level's part of U",
            qs_done="VectorE: q times exp(decay)",
            z_done="ScalarE: silu(z)",
            gc_done="ScalarE: silu of retention's gate",
            gn_done="ScalarE: 1 / norm of heads' outputs",
            gated="VectorE: normed and gated outputs",
            maxima="VectorE: minus the rows' maxima",
            exps="ScalarE: exponentials and sums",
            probs="VectorE: a head's probabilities",
            rope_done="VectorE: a block rotated",
            upper_half="TensorE: scores of the heads in rows 0 to 63",
            qd_done="VectorE: retention's q times its decay",
            oc_sq="ScalarE: squares of retention's centred output",
            bias_masked="GpSimd: the bias tile is complete",
            opening="GpSimd: every engine has arrived",
            act_step="ScalarE: any other instruction of its own",
            dve_step="VectorE: likewise",
            pool_step="GpSimd: likewise",
        )
        names = list(signals)
        S = {n: sem(n) for n in names}
        filled = [sem(f"filled{i}") for i in range(4)]
        drained = [sem(f"drained{i}") for i in range(4)]
        cleared = [*map(S.get, names), *filled, *drained]
        first, last = cleared[0].num, cleared[-1].num
        assert last - first == len(cleared) - 1
        for n in ("y_normed", "y_turned", "y_out", "y_stored"):
            S[n] = sem(n)
        first_load = sem("first_load")
        x_turned = sem("x_turned")
        x_in = sem("x_in")

        def small(key):
            return psum[:, 4 + USE[key][0], :]

        def open_bank(pe, key):
            k, n = USE[key]
            if n:
                pe.wait_ge(drained[k], n)

        def fill(ins, key):
            ins.then_inc(filled[USE[key][0]], 1)

        def wait_filled(eng, key):
            k, n = USE[key]
            eng.wait_ge(filled[k], n + 1)

        def wait_drained(eng, key):
            k, n = USE[key]
            eng.wait_ge(drained[k], n + 1)

        class Engine:

            def __init__(self, eng, step):
                self.eng, self.step, self.counts = eng, step, {}

            def do(self, ins, name=None):
                name = name or self.step
                self.counts[name] = self.counts.get(name, 0) + 1
                ins.then_inc(S[name], 1)
                self.eng.wait_ge(S[name], self.counts[name])

            def drain(self, ins, key):
                k, n = USE[key]
                ins.then_inc(drained[k], 1)
                self.eng.wait_ge(drained[k], n + 1)

            def do_at(self, ins, s, value):
                ins.then_inc(s, 1)
                self.eng.wait_ge(s, value)

        def in_turn(eng, first, blocks, last, body):
            for n in range(first):
                body(n, 0)
            assert (blocks - first - last) % 2 == 0
            with eng.Fori(0, (blocks - first - last) // 2) as i:
                body(first, i)
                body(first + 1, i)
            for n in range(blocks - last, blocks):
                body(n, 0)

        def tap(b, j):
            return par[:, R_CONV + j * CB + b:R_CONV + j * CB + b + 1]

        block = ctx.enter_context(nc.Block())

        @block.sync
        def _(sp):
            def load(layer, u, i, src):
                sp.wait_ge(lo_done, layer * UNITS + 4 * i + u + 1)
                n = src.shape[1] * src.shape[2]
                dst = raw[:, u % RAW, 0:n].rearrange("p (k c) -> p k c", k=src.shape[1])
                sp.dma_start(dst, src).then_inc(landed[u % RAW], 16)

            def view(w, layer, row0, rows, col, cols):
                return w[bass.ds(layer, 1), row0:row0 + rows, bass.ds(col, cols)].rearrange(
                    "a (k p) c -> p (a k) c", p=P)

            def ffn_units(layer, u0, wg, wu, wd):
                def gate_up(j, i):
                    u = u0 + 2 * j
                    load(layer, u, i, view(wg, layer, 0, D_MODEL, (2 * i + j) * 256, 256))
                    load(layer, u + 1, i, view(wu, layer, 0, D_MODEL, (2 * i + j) * 256, 256))

                def down(b, i):
                    u = u0 + 2 * NJ + 2 * b
                    for r in range(2):
                        load(layer, u + r, i, view(wd, layer, r * DOWN_K * P, DOWN_K * P, (2 * i + b) * P, P))

                in_turn(sp, 1, NJ, 0, gate_up)
                in_turn(sp, 2, KD, 2, down)

            for t in range(2):
                sp.dma_start(tok[:, t, :], x_prompt[0, t * P:(t + 1) * P, :]).then_inc(first_load, 16)
            sp.dma_start(tok[0:DEC, 2, :], x_sample[0]).then_inc(first_load, 16)
            with sp.Fori(0, DEPTH) as layer:
                ffn_units(layer, U_FFN1, w_g1, w_u1, w_d1)
                for n, (kind, _, col) in enumerate(IN_UNITS):
                    load(layer, U_IN + n, 0, view(w_in, layer, 0, D_MODEL, col, P if kind == "tail" else 256))
                for d in range(4):
                    load(layer, U_OUT + d, 0, view(w_out, layer, 0, D_MODEL, d * 256, 256))
                ffn_units(layer, U_FFN2, w_g2, w_u2, w_d2)

        @block.gpsimd
        def _(pool):
            pool.memset(spare[:, 3:4], 0.0).then_inc(lo_done, RAW)
            pool.wait_ge(lo_done, RAW)
            pool.memset(spare[:, 4:5], 0.0).then_inc(unit_used, SPLIT)
            pool.wait_ge(unit_used, SPLIT)

            def idle(n):
                return pool.tensor_tensor(spare[:, n:n + 1], C("eps"), C("eps"), ALU.add)

            pool.wait_ge(first_load, 64)

            def low_parts(norm, me):
                for k in range(KD):
                    pool.wait_ge(S["hh_done"], norm * KD + k + 1)
                    me.do(pool.tensor_tensor(hl[:, k, :], tmp[:, k, 0:T], hh[:, k, :].bitcast(F32), ALU.subtract),
                          "hl_done")

            def add_squares(f, me):
                def add(n, i):
                    if 0 < n < KD - 1:
                        pool.wait_ge(S["sq_done"], SQ0[f] + 2 * i + n + 1)
                        block = tmp[:, bass.ds(2 * i + n, 1), 0:T].rearrange("p a t -> p (a t)")
                        me.do_at(pool.tensor_tensor(tmp[:, 0, 0:T], tmp[:, 0, 0:T], block, ALU.add), S["squares_added"],
                                 ADD0[f] + 2 * i + n)

                in_turn(pool, 2, KD, 2, add)

            with pool.Fori(0, DEPTH) as layer:
                pool.wait_ge(arrived, 3 * layer + 3)
                idle(0).then_inc(S["opening"], 1)
                pool.wait_ge(S["opening"], 1)
                pool.sem_clear(range(first, last + 1))
                pool.memset(spare[:, 2:3], 0.0).then_inc(layer_open, 1)
                me = Engine(pool, "pool_step")
                low_parts(0, me)

                for w, dst in ((a_log, ea), (dt_bias, dtb)):
                    pool.dma_start(dst[:, :], w[bass.ds(layer, 1)].to_broadcast([P, H])).then_inc(gate_loaded, 16)
                pool.dma_start(sS[:, :, :], state_gdn[bass.ds(layer, 1)].rearrange("a e h k v -> k (a e h) v")
                               ).then_inc(state_loaded, 16)
                pool.dma_start(sR[:, :, :], state_ret[bass.ds(layer, 1)].rearrange("a e (b c) k v -> (a e c k) b v", c=2)
                               ).then_inc(state_loaded, 16)
                for w, dst in ((cache_k, ck), (cache_v, cv)):
                    pool.dma_start(dst[:, :], w[bass.ds(layer, 1)].rearrange("a e t h d -> (a e t) (h d)")
                                   ).then_inc(cache_loaded, 16)
                row = bias[0:H, :, :].rearrange("p h x -> p (h x)")[:, 0:384]
                pool.dma_start(row[:, P:384], rel_bias[bass.ds(layer, 1), :, 0:256].rearrange("a h o -> (a h) o")
                               ).then_inc(row_loaded, 16)
                pool.wait_ge(row_loaded, (layer + 1) * 16)
                me.do(idle(5))
                me.do(pool.tensor_scalar(row[:, 0:P], C("ones", H), row[:, P:P + 1], None, ALU.mult))
                pool.dma_start(bias_copies.rearrange("p h x -> h p x"), row[:, None, :].to_broadcast([H, P, 384])
                               ).then_inc(copies_stored, 16)
                pool.wait_ge(copies_stored, (layer + 1) * 16)
                me.do(idle(5))
                pool.dma_start(bias[:, :, :], bass.AP(bias_copies, P, [[H * 384 - 1, P], [384, H], [1, 256]])
                               ).then_inc(bias_loaded, 16)
                pool.wait_ge(bias_loaded, (layer + 1) * 16)
                me.do(idle(5))
                me.do(pool.memset(bias[0:64, :, 192:256], NEG), "bias_masked")

                add_squares(0, me)
                low_parts(1, me)
                stores = 0

                def store(dst, src):
                    nonlocal stores
                    pool.dma_start(dst, src).then_inc(stored, 16)
                    stores += 16

                one = bass.ds(layer, 1)
                for step in STEPS:
                    if step[0] == "D":
                        t = step[1]
                        L = TILES[t][2]
                        ug, bi = B[t]["Us"], B[t]["Vn"]
                        pool.wait_ge(S["gates_done"], 1)
                        if t == 2:
                            wait_drained(pool, ("Zt", 1, LEVELS[1][-1]))
                        for h in range(H):
                            me.do(pool.tensor_scalar(ug[0:L, h, 0:L], C("utri", L, L), gt[0:L, G, t, h:h + 1], None,
                                                     ALU.mult))
                            me.do(pool.tensor_scalar(bi[0:L, h, 0:L], C("ident", L, L), gt[0:L, BETA, t, h:h + 1],
                                                     None, ALU.mult), "spread" if h == H - 1 else None)
                    elif step[0] == "conv":
                        i = step[1]
                        pool.wait_ge(S["unit_out"], CONV_UNIT[i] + 1)
                        slot = 2 * (i % 2)
                        for s, end in enumerate((PAD + SEQ, UPW)):
                            me.do(pool.tensor_copy(lastc[:, s, :, 2 * i:2 * i + 2].rearrange("p r b -> p b r"),
                                                   up[:, slot:slot + 2, end - PAD:end]), "last_kept" if s else None)
                    elif step[0] == "split":
                        k = SPLIT_ORDER[step[1]]
                        pool.wait_ge(S["hh_done"], 2 * KD + step[1] + 1)
                        me.do(pool.tensor_tensor(hl[:, k, :], tmp[:, k, 0:T], hh[:, k, :].bitcast(F32), ALU.subtract),
                              "hl_done")
                    elif step == ("btok", 2):
                        wait_drained(pool, step)
                        for w, src in ((p_k, btk), (p_v, btv)):
                            store(w[one].rearrange("a e (t p) h d -> p (a e t) (h d)", p=P), src[:, 0:2, :])
                        for w, src in ((s_k, btk), (s_v, btv)):
                            store(w[one].rearrange("a e p h d -> (a e p) (h d)"), src[0:DEC, 2, :])
                    elif step[0] == "lc":
                        wait_drained(pool, step)
                        for s, w in enumerate((p_conv, s_conv)):
                            store(w[one].rearrange("a e r (b p) -> (a e r b) p", p=P),
                                  lastr[s * PAD * CB:(s + 1) * PAD * CB, :])
                    elif step in (("Su", 1), ("Su", 2)):
                        wait_drained(pool, step)
                        store((p_gdn if step[1] == 1 else s_gdn)[one].rearrange("a e h k v -> k (a e h) v"),
                              (pS if step[1] == 1 else sS)[:, :, :])
                    elif step in (("R", 1), ("R", 2)):
                        wait_drained(pool, step)
                        store((p_ret if step[1] == 1 else s_ret)[one].rearrange("a e (b c) k v -> (a e c k) b v", c=2),
                              (pR if step[1] == 1 else sR)[:, :, :])
                assert stores == 16 * STORES
                for d in (1, 2):
                    pool.wait_ge(S["sq_done"], SQ_OUT + d + 1)
                    me.do_at(pool.tensor_tensor(tmp[:, 0:2, 0:T], tmp[:, 0:2, 0:T], tmp[:, 2 * d:2 * d + 2, 0:T], ALU.add),
                             S["squares_added"], ADD_OUT + d)
                low_parts(3, me)
                add_squares(1, me)
                pool.wait_ge(stored, (layer + 1) * stores)
                me.do(idle(5))
            for t in range(3):
                pool.wait_ge(S["y_out"], 2 * t + 2)
                if t < 2:
                    pool.dma_start(y_prompt[0, t * P:(t + 1) * P, :], tok[:, t, :]).then_inc(S["y_stored"], 16)
                else:
                    pool.dma_start(y_sample[0], tok[0:DEC, 2, :]).then_inc(S["y_stored"], 16)
            pool.wait_ge(S["y_stored"], 48)

        @block.tensor
        def _(pe):
            def products(layer, u, i, nk, nb, hi, lo, banks, k0=0, start=True, stop=True, before=None):
                pe.wait_ge(lo_done, layer * UNITS + 4 * i + u + 1 + RAW)
                s, width = u % SPLIT, nb * P
                for k in range(nk):
                    if before:
                        before(k)
                    for b in range(nb):
                        out = psum[:, banks[b], 0:T]
                        at = k * width + b * P
                        wh, wl = whi[:, s, at:at + P], wlo[:, s, at:at + P]
                        pe.matmul(out, wh, hi[:, k0 + k, :], start=start and k == 0, stop=False)
                        pe.matmul(out, wh, lo[:, k0 + k, :], start=False, stop=False)
                        mm = pe.matmul(out, wl, hi[:, k0 + k, :], start=False, stop=stop and k == nk - 1)
                mm.then_inc(unit_used, 1)

            def input_ready(norm):
                return lambda k: pe.wait_ge(S["hl_done"], norm * KD + k + 1)

            def ffn_products(layer, u0, f, norm):
                def gate_up(n, i):
                    u = u0 + 2 * n
                    if n:
                        pe.wait_ge(S["gate_silu"], NJ * f + 2 * i + n)
                    products(layer, u, i, KD, 2, hh, hl, (0, 1), before=None if n else input_ready(norm))
                    if n:
                        pe.wait_ge(S["product"], NJ * f + 2 * i + n)
                    products(layer, u + 1, i, KD, 2, hh, hl, (2, 3))

                def act_ready(k0):
                    return lambda k: pe.wait_ge(S["act_lo_done"], NJ * f + (k0 + k) // 2 + 1)

                def down(n, i):
                    u = u0 + 2 * NJ + 2 * n
                    if n == 0:
                        pe.wait_ge(S["gate_silu"], NJ * f + NJ)
                    if n >= 2:
                        pe.wait_ge(S["x_updated"], SQ0[f] + 2 * i + n - 1)
                    products(layer, u, i, DOWN_K, 1, act_hi, act_lo, (n % 2,), stop=False,
                             before=None if n else act_ready(0))
                    products(layer, u + 1, i, DOWN_K, 1, act_hi, act_lo, (n % 2,), k0=DOWN_K, start=False,
                             before=None if n else act_ready(DOWN_K))

                stat = ("stat", 2 * f)
                in_turn(pe, 1, NJ, 0, gate_up)
                in_turn(pe, 2, KD, 2, down)
                open_bank(pe, stat)
                pe.wait_ge(S["squares_added"], ADD0[f] + KD - 2)
                pe.matmul(small(stat)[:, 0:T], C("ones"), tmp[:, 0, 0:T], start=True, stop=False)
                pe.wait_ge(S["sq_done"], SQ0[f] + KD)
                fill(pe.matmul(small(stat)[:, 0:T], C("ones"), tmp[:, KD - 1, 0:T], start=False, stop=True), stat)

            def heads(key, L, width, lhs, rhs):
                bank = small(key)
                for h in range(H):
                    mm = pe.matmul(bank[0:L, h * width:(h + 1) * width], lhs(h), rhs(h), start=True, stop=True)
                fill(mm, key)

            def turn(out, src):
                n = src.shape[0]
                return pe.transpose(out, src, C("ident", n, n))

            pe.wait_ge(first_load, 64)
            for k in range(KD):
                for t, (c0, _, L) in enumerate(TILES):
                    mm = turn(psum[:, k, c0:c0 + L], tok[0:L, t, k * P:(k + 1) * P])
                mm.then_inc(x_turned, 1)
            for k in range(KD):
                pe.wait_ge(x_in, 2 * k + 2)
                mm = pe.matmul(psum[:, 0, 0:T], C("ones"), tmp[:, k, 0:T], start=k == 0, stop=k == KD - 1)
            mm.then_inc(x_turned, 1)
            pe.wait_ge(par_loaded, PAR_LOADS * 16)
            for n in range(DEPTH):
                turn(psum[:, 5 + n, 0:NPAR], parrow[:, n, :]).then_inc(par_turned, 1)

            with pe.Fori(0, DEPTH) as layer:
                pe.drain().then_inc(arrived, 1)
                pe.wait_ge(layer_open, layer + 1)
                ffn_products(layer, U_FFN1, 0, 0)

                for step in STEPS:
                    kind, t = step[0], (step[1] if len(step) > 1 else None)
                    if kind == "part":
                        part, s = step[2], (U_IN + t) % SPLIT
                        if part == 0:
                            pe.wait_ge(lo_done, layer * UNITS + U_IN + t + 1 + RAW)
                            if t >= 2:
                                pe.wait_ge(S["unit_out"], t - 1)
                        nb = 1 if IN_UNITS[t][0] == "tail" else 2
                        ks = KD // (2 * nb)
                        for k in range(part * ks, part * ks + ks):
                            if t == 0:
                                pe.wait_ge(S["hl_done"], KD + k + 1)
                            for b in range(nb):
                                out = psum[:, 2 * (t % 2) + b, 0:T]
                                at = (k * nb + b) * P
                                wh, wl = whi[:, s, at:at + P], wlo[:, s, at:at + P]
                                pe.matmul(out, wh, hh[:, k, :], start=k == 0, stop=False)
                                pe.matmul(out, wh, hl[:, k, :], start=False, stop=False)
                                mm = pe.matmul(out, wl, hh[:, k, :], start=False, stop=k == KD - 1)
                        if part == 2 * nb - 1:
                            mm.then_inc(unit_used, 1)
                    if kind == "project":
                        if t == 0:
                            pe.wait_ge(lo_done, layer * UNITS + U_OUT + 1 + RAW)
                            pe.wait_ge(S["unit_out"], 15)
                        pe.wait_ge(S["hl_done"], 2 * KD + t + 1)
                        for b in range(2):
                            k, out, s = SPLIT_ORDER[t], psum[:, b, 0:T], U_OUT % SPLIT
                            at = (2 * k + b) * P
                            wh, wl = whi[:, s, at:at + P], wlo[:, s, at:at + P]
                            pe.matmul(out, wh, hh[:, k, :], start=t == 0, stop=False)
                            pe.matmul(out, wh, hl[:, k, :], start=False, stop=False)
                            mm = pe.matmul(out, wl, hh[:, k, :], start=False, stop=t == KD - 1)
                        if t == KD - 1:
                            mm.then_inc(unit_used, 1)
                    if kind in NO_BANK:
                        continue
                    if kind != "Z":
                        open_bank(pe, step)
                        bank = small(step)
                    if kind in PER_TILE:
                        c0, p0, L = TILES[t]
                        vb, kt, aT, Vt, U, Us, Vn, Ysb, lm = map(B[t].get, BUFFERS)
                        ug, bi = Us, Vn
                        q = lambda h: qkv[:, h, p0:p0 + L]
                        k = lambda h: qkv[:, H + h, p0:p0 + L]
                        state, rstate = (pS, pR) if t < 2 else (sS, sR)
                    if kind in ("sA", "sB", "pT", "oB"):
                        b, r = t // 2, slice(64 * (t % 2), 64 * (t % 2) + 64)
                    if kind == "ba":
                        pe.wait_ge(S["unit_out"], 5)
                        for n, (c0, _, L) in enumerate(TILES):
                            mm = turn(bank[0:L, 8 * n:8 * n + 8], baT[:, c0:c0 + L])
                        fill(mm, step)
                    elif kind == "ss":
                        pe.wait_ge(S["sq2_done"], t + 1)
                        fill(pe.matmul(bank[:, 0:CW], C("ones"), tmp[:, t, :], start=True, stop=True), step)
                    elif kind == "dcol":
                        pe.wait_ge(S["gates_done"], 1)
                        for n, (_, _, L) in enumerate(TILES):
                            mm = pe.matmul(bank[0:L, H * n:H * n + H], C("utri", L, L), gt[0:L, G, n, :],
                                           start=True, stop=True)
                        fill(mm, step)
                    elif kind == "vt":
                        pe.wait_ge(S["silu_done"], 6)
                        for h in range(H):
                            mm = turn(bank[0:L, h * P:(h + 1) * P], qkv[:, 2 * H + h, p0:p0 + L])
                        fill(mm, step)
                    elif kind == "D":
                        pe.wait_ge(S["spread"], t + 1)
                        fill(pe.matmul(bank[:, 0:H * L].rearrange("p (h l) -> p h l", h=H), C("ones", L),
                                       ug[0:L, :, 0:L], start=True, stop=True), step)
                    elif kind == "Bb":
                        fill(pe.matmul(bank[0:L, 0:H * L].rearrange("p (h l) -> p h l", h=H), C("ones", L, L),
                                       bi[0:L, :, 0:L], start=True, stop=True), step)
                    elif kind == "G":
                        pe.wait_ge(S["qk_normed"], 8)
                        heads(step, L, L, k, k)
                    elif kind == "QK":
                        heads(step, L, L, k, q)
                    elif kind == "kt":
                        for h in range(H):
                            mm = turn(bank[0:L, h * P:(h + 1) * P], k(h))
                        fill(mm, step)
                    elif kind == "T1":
                        pe.wait_ge(S["tri_done"], t + 1)
                        for h in range(H):
                            mm = turn(bank[0:L, h * L:(h + 1) * L], Vt[0:L, h, 0:L])
                        fill(mm, step)
                    elif kind == "Y":
                        s = step[2]
                        if s == LEVELS[t][0]:
                            wait_drained(pe, ("T1", t))
                        else:
                            pe.wait_ge(S["level_done"], LEVEL_DONE[t, s // 2])
                            wait_drained(pe, ("Zt", t, s // 2))
                            wait_drained(pe, ("Z", t, s // 2))
                        heads(step, L, L, lambda h: Us[0:L, h, 0:L], lambda h: Vn[0:L, h, 0:L])
                    elif kind == "Z":
                        s = step[2]
                        wait_drained(pe, ("Y", t, s))
                        open_bank(pe, ("Zt", t, s))
                        heads(("Zt", t, s), L, L, lambda h: Ysb[0:L, h, 0:L], lambda h: Vt[0:L, h, 0:L])
                        if s != LEVELS[t][-1]:
                            open_bank(pe, step)
                            heads(step, L, L, lambda h: Vt[0:L, h, 0:L], lambda h: Ysb[0:L, h, 0:L])
                    elif kind == "kS":
                        heads(step, L, P, k, lambda h: state[:, h, :])
                    elif kind == "vn":
                        wait_drained(pe, ("Zt", t, LEVELS[t][-1]))
                        wait_drained(pe, ("kS", t) if t else ("vt", t))
                        heads(step, L, P, lambda h: Vt[0:L, h, 0:L], lambda h: vb[0:L, h, :])
                    elif kind == "o":
                        wait_drained(pe, ("vn", t))
                        if t:
                            pe.wait_ge(S["qs_done"], t)
                        for h in range(H):
                            if t:
                                pe.matmul(bank[:, h * L:(h + 1) * L], state[:, h, :], q(h), start=True, stop=False)
                            mm = pe.matmul(bank[:, h * L:(h + 1) * L], vn[0:L, h, :], aT[0:L, h, 0:L],
                                           start=t == 0, stop=True)
                        fill(mm, step)
                    elif kind == "Su":
                        wait_drained(pe, ("kt", t))
                        heads(step, P, P, lambda h: kt[0:L, h, :], lambda h: vn[0:L, h, :])
                    elif kind == "on":
                        wait_drained(pe, ("o", t))
                        fill(pe.matmul(bank[:, 0:H * L], C("ones"), osq[:, 0:H * L], start=True, stop=True), step)
                    elif kind == "btok":
                        pe.wait_ge(S["unit_out"], 10)
                        for b in range(2):
                            turn(bank[0:L, b * P:(b + 1) * P], bk[:, b, c0:c0 + L])
                            mm = turn(bank[0:L, 256 + b * P:256 + (b + 1) * P], bv[:, b, c0:c0 + L])
                        fill(mm, step)
                    elif kind == "bkc":
                        pe.wait_ge(cache_loaded, (layer + 1) * 32)
                        pe.wait_ge(state_loaded, (layer + 1) * 32)
                        for b in range(2):
                            mm = turn(bank[:, b * P:(b + 1) * P], ck[:, b * P:(b + 1) * P])
                        fill(mm, step)
                    elif kind == "lc":
                        pe.wait_ge(S["last_kept"], 6)
                        fill(turn(bank[0:2 * PAD * CB, 0:P], lastc[:, :, :, :].rearrange("p s r b -> p (s r b)")), step)
                    elif kind == "sA":
                        pe.matmul(bank[:, 0:P], bq[r, b, 0:P], bk[r, b, 0:P], start=True, stop=True)
                        fill(pe.matmul(bank[:, P:3 * P], bq[r, b, P:2 * P], bk[r, b, 0:2 * P], start=True, stop=True), step)
                    elif kind == "sB":
                        wait_drained(pe, ("bkc",))
                        pe.matmul(bank[0:DEC, 0:P], bq[r, b, SEQ:T], kcT[r, b, :], start=True, stop=True)
                        fill(pe.matmul(bank[0:DEC, P:P + DEC], bq[r, b, SEQ:T], bk[r, b, SEQ:T], start=True, stop=True),
                             step)
                    elif kind == "pT":
                        pe.wait_ge(S["probs"], t + 1)
                        for n in range(3):
                            turn(bank[:, n * P:(n + 1) * P], prob[:, n * P:(n + 1) * P])
                        turn(bank[:, 384:448], prob[0:DEC, 384:512])
                        fill(turn(bank[0:DEC, 448:512], prob[0:DEC, 512:576]), step)
                    elif kind == "oB":
                        wait_drained(pe, ("pT", t))
                        wait_drained(pe, ("btok", 2))
                        v = slice(64 * t, 64 * t + 64)
                        pe.matmul(bank[r, 0:128], btv[:, 0, v], pT[:, 0:128], start=True, stop=True)
                        pe.matmul(bank[r, 128:256], btv[:, 0, v], pT[:, 128:256], start=True, stop=False)
                        pe.matmul(bank[r, 128:256], btv[:, 1, v], pT[:, 256:384], start=False, stop=True)
                        pe.matmul(bank[r, 256:320], cv[:, v], pT[:, 384:448], start=True, stop=False)
                        fill(pe.matmul(bank[r, 256:320], btv[0:DEC, 2, v], pT[0:DEC, 448:512], start=False, stop=True), step)
                    elif kind == "rot":
                        pe.wait_ge(S["unit_out"], 13 + t // 2)
                        fill(pe.matmul(bank[:, 0:T], C("rot"), (bq, bk)[t // 2][:, t % 2, :], start=True, stop=True), step)
                    elif kind == "ctok":
                        pe.wait_ge(S["rope_done"], 4)
                        pe.wait_ge(S["unit_out"], 15)
                        for b in range(2):
                            turn(bank[0:L, b * P:(b + 1) * P], bk[:, b, c0:c0 + L])
                            mm = turn(bank[0:L, 256 + b * P:256 + (b + 1) * P], bv[:, b, c0:c0 + L])
                        fill(mm, step)
                    elif kind == "cqk":
                        for h in (0, 2, 1, 3):
                            b, r = h // 2, slice(64 * (h % 2), 64 * (h % 2) + 64)
                            mm = pe.matmul(bank[0:L, h * L:(h + 1) * L], bk[r, b, c0:c0 + L], bq[r, b, c0:c0 + L],
                                           start=True, stop=True)
                            if h == 2:
                                mm.then_inc(S["upper_half"], 1)
                                pe.wait_ge(S["upper_half"], t + 1)
                        fill(mm, step)
                    elif kind == "oC":
                        wait_drained(pe, ("cqk", t))
                        wait_drained(pe, ("ctok", t))
                        if t:
                            pe.wait_ge(S["qd_done"], t)
                            wait_drained(pe, ("R", t - 1))
                        for h in range(H):
                            b, r = h // 2, slice(64 * (h % 2), 64 * (h % 2) + 64)
                            out = bank[r, b * P:b * P + L]
                            if t:
                                pe.matmul(out, rstate[r, b, :], bq[r, b, c0:c0 + L], start=True, stop=False)
                            mm = pe.matmul(out, ctv[:, 64 * h:64 * h + 64], aC[:, h, 0:L], start=t == 0, stop=True)
                        fill(mm, step)
                    elif kind == "R":
                        for h in range(H):
                            b, r = h // 2, slice(64 * (h % 2), 64 * (h % 2) + 64)
                            v = slice(64 * h, 64 * h + 64)
                            mm = pe.matmul(bank[r, b * 64:b * 64 + 64], ctk[0:L, v], ctv[0:L, v], start=True, stop=True)
                        fill(mm, step)
                    elif kind == "cm":
                        wait_drained(pe, ("oC", 2))
                        fill(pe.matmul(bank[:, 0:T], C("mean64"), oC[:, t, :], start=True, stop=True), step)
                    elif kind == "cv":
                        pe.wait_ge(S["oc_sq"], t + 1)
                        fill(pe.matmul(bank[:, 0:T], C("mean64"), tmp[:, 6 + t, 0:T], start=True, stop=True), step)

                stat = ("stat", 1)

                for d in range(1, 4):
                    if d >= 2:
                        pe.wait_ge(S["x_updated"], SQ_OUT + d - 1)
                    else:
                        pe.wait_ge(S["unit_out"], 16)
                    products(layer, U_OUT + d, 0, KD, 2, hh, hl, (2 * (d % 2), 2 * (d % 2) + 1))
                open_bank(pe, stat)
                pe.wait_ge(S["squares_added"], ADD_OUT + 2)
                for b in (0, 1):
                    pe.matmul(small(stat)[:, 0:T], C("ones"), tmp[:, b, 0:T], start=b == 0, stop=False)
                pe.wait_ge(S["sq_done"], SQ_OUT + 4)
                for b in (6, 7):
                    mm = pe.matmul(small(stat)[:, 0:T], C("ones"), tmp[:, b, 0:T], start=False, stop=b == 7)
                fill(mm, stat)
                ffn_products(layer, U_FFN2, 1, 3)

            pe.wait_ge(S["y_normed"], KD)
            for t, (c0, _, L) in enumerate(TILES):
                for half in range(2):
                    for n in range(4):
                        mm = turn(psum[0:L, 2 * t + half, n * P:(n + 1) * P], tmp[:, 4 * half + n, c0:c0 + L])
                    mm.then_inc(S["y_turned"], 1)

        @block.scalar
        def _(act):
            A = act.activation

            def split_hi(layer, u, i=0, width=SLOT):
                act.wait_ge(landed[u % RAW], (layer * (UNITS // RAW) + i + u // RAW + 1) * 16)
                act.wait_ge(unit_used, layer * UNITS + 4 * i + u + 1)
                ins = A(whi[:, u % SPLIT, 0:width], raw[:, u % RAW, 0:width], ACT.Copy)
                ins.then_inc(hi_done, 1)
                act.wait_ge(hi_done, layer * UNITS + 4 * i + u + 1)

            def wait_products(layer, u, i=0):
                act.wait_ge(unit_used, layer * UNITS + 4 * i + u + 1 + SPLIT)

            def rsqrt(dst, src, scale, me, key, name, extra=0.0):
                me.drain(A(dst, src, ACT.Ln, bias=C("eps"), scale=scale), key)
                me.do(A(dst, dst, ACT.Exp, bias=extra, scale=-0.5), name)

            def ffn(layer, u0, f, norm, me):
                def gate_up(n, i):
                    u = u0 + 2 * n
                    at = bass.ds(2 * (2 * i + n), 2)
                    split_hi(layer, u + 1, i)
                    wait_products(layer, u, i)
                    if n:
                        act.wait_ge(S["product"], NJ * f + 2 * i + n)
                    me.do_at(A(gs[:, :, :], psum[:, 0:2, 0:T], ACT.Silu), S["gate_silu"], NJ * f + 2 * i + n + 1)
                    split_hi(layer, u + 2, i)
                    act.wait_ge(S["product"], NJ * f + 2 * i + n + 1)
                    me.do_at(A(act_hi[:, at, :], prod[:, :, :], ACT.Copy), S["act_hi_done"], NJ * f + 2 * i + n + 1)

                def down(n, i):
                    u = u0 + 2 * NJ + 2 * n
                    for r in range(2):
                        if u + r + 1 < UNITS:
                            split_hi(layer, u + r + 1, i, SLOT if n == KD - 1 and r else DOWN_K * P)
                    act.wait_ge(S["x_updated"], SQ0[f] + 2 * i + n + 1)
                    at = bass.ds(2 * i + n, 1)
                    me.do_at(A(tmp[:, at, 0:T], xT[:, at, :], ACT.Square), S["sq_done"], SQ0[f] + 2 * i + n + 1)

                in_turn(act, 1, NJ, 0, gate_up)
                act.preload_act_table_set(LN_EXP)
                in_turn(act, 2, KD, 2, down)

            def apply_norm(norm, hf, me):
                for k in range(KD):
                    act.wait_ge(S["hf_done"], hf * KD + k + 1)
                    me.do(A(hh[:, k, :], tmp[:, k, 0:T], ACT.Copy), "hh_done")

            def statistics(i, me):
                key = ("stat", i)
                wait_filled(act, key)
                rsqrt(rstd[:, :], small(key)[:, 0:T], 1.0 / D_MODEL, me, key, "rstd_done")

            act.dma_start(cst[:, 0:FIRST_CONSTS], consts[:, 0:FIRST_CONSTS]).then_inc(first_load, 16)
            for w, at, n in ((norm_ffn1, R_F1, 8), (norm_mix, R_MIX, 8), (norm_ffn2, R_F2, 8), (gdn_norm, R_GDN, 1)):
                act.dma_start(parrow[at:at + n, :, :], w.rearrange("a (b p) -> b a p", p=P)).then_inc(par_loaded, 16)
            act.dma_start(parrow[R_CONV:R_CONV + 4 * CB, :, :], conv_w.rearrange("a j (b p) -> (j b) a p", p=P)
                          ).then_inc(par_loaded, 16)
            act.dma_start(parrow[R_STATE:R_STATE + PAD * CB, :, :],
                          state_conv.rearrange("a e j (b p) -> (e j b) a p", p=P)).then_inc(par_loaded, 16)
            act.dma_start(parrow[R_FINAL:R_FINAL + 8, :, :],
                          norm_final.rearrange("(b p) -> b p", p=P)[:, None, :].to_broadcast([8, DEPTH, P])
                          ).then_inc(par_loaded, 16)
            act.dma_start(cst[:, FIRST_CONSTS:], consts[:, FIRST_CONSTS:]).then_inc(par_loaded, 16)
            act.wait_ge(first_load, 64)
            n = 0
            for k in range(KD):
                act.wait_ge(x_turned, k + 1)
                for dst, src, f in ((xT[:, k, :], psum[:, k, 0:T], ACT.Copy), (tmp[:, k, 0:T], xT[:, k, :], ACT.Square)):
                    A(dst, src, f).then_inc(x_in, 1)
                    n += 1
                    act.wait_ge(x_in, n)
            act.preload_act_table_set(LN_EXP)
            act.wait_ge(x_turned, KD + 1)
            A(rstd[:, :], psum[:, 0, 0:T], ACT.Ln, bias=C("eps"), scale=1.0 / D_MODEL).then_inc(x_in, 1)
            act.wait_ge(x_in, n + 1)
            A(rstd[:, :], rstd[:, :], ACT.Exp, scale=-0.5).then_inc(x_in, 1)
            act.wait_ge(x_in, n + 2)

            with act.Fori(0, DEPTH) as layer:
                act.drain().then_inc(arrived, 1)
                split_hi(layer, 0)
                act.wait_ge(layer_open, layer + 1)
                me = Engine(act, "act_step")
                me.do(A(spare[:, 1:2], C("eps"), ACT.Copy))
                apply_norm(0, 0, me)
                ffn(layer, U_FFN1, 0, 0, me)
                statistics(0, me)
                apply_norm(1, 1, me)

                for step in STEPS:
                    kind, t = step[0], (step[1] if len(step) > 1 else None)
                    if kind in PER_TILE:
                        c0, p0, L = TILES[t]
                        vb, kt, aT, Vt, U, Us, Vn, Ysb, lm = map(B[t].get, BUFFERS)
                        wide = lambda x: x[:, 0:H * L].rearrange("p (h l) -> p h l", h=H)
                    if kind == "hi":
                        tail = t < len(IN_UNITS) and IN_UNITS[t][0] == "tail"
                        split_hi(layer, U_IN + t, 0, KD * P if tail else SLOT)
                    elif kind == "silu":
                        act.wait_ge(S["conv_done"], t + 1)
                        me.do(A(qkv[:, 2 * t:2 * t + 2, :], qkv[:, 2 * t:2 * t + 2, :], ACT.Silu), "silu_done")
                        if t == CB // 2 - 1:
                            act.preload_act_table_set(LN_EXP)
                    elif kind == "out":
                        wait_products(layer, U_IN + t)
                        what, i, _ = IN_UNITS[t]
                        src = psum[:, 2 * (t % 2):2 * (t % 2) + 2, 0:T]
                        if what == "conv":
                            slot = 2 * (i % 2)
                            if i >= 2:
                                act.wait_ge(S["conv_done"], i - 1)
                                act.wait_ge(S["last_kept"], i - 1)
                            me.do(A(up[:, slot:slot + 2, PAD:PAD + SEQ], src[:, :, 0:SEQ], ACT.Copy))
                            me.do(A(up[:, slot:slot + 2, PAD + SEQ + PAD:UPW], src[:, :, SEQ:T], ACT.Copy))
                            state = par[:, R_STATE:R_STATE + PAD * CB].rearrange("p (r b) -> p b r", r=PAD)
                            me.do(A(up[:, slot:slot + 2, PAD + SEQ:PAD + SEQ + PAD], state[:, 2 * i:2 * i + 2, :], ACT.Copy))
                            act.wait_ge(S["pads_zero"], 1)
                            for c in range(2):
                                b = 2 * i + c
                                me.do(A(qkv[:, b, :], up[:, slot + c, 0:CW], ACT.Copy, scale=tap(b, 0)),
                                      "unit_out" if c else None)
                        elif what == "tail":
                            me.do(A(baT[:, :], src[0:8, 0, :], ACT.Copy), "unit_out")
                        else:
                            if what == "z":
                                act.wait_ge(S["conv_done"], 6)
                                act.wait_ge(S["last_kept"], 6)
                                dst = z[:, 2 * i:2 * i + 2, :]
                            else:
                                dst = dict(qb=bq, kb=bk, vb=bv, qc=bq, kc=bk, vc=bv, gc=gc)[what][:, :, :]
                            me.do(A(dst, src, ACT.Copy), "unit_out")
                    elif kind == "sq":
                        me.do(A(tmp[:, t, :], qkv[:, t, :], ACT.Square), "sq2_done")
                    elif kind == "exps":
                        act.wait_ge(S["gates_in"], 1)
                        me.do(A(gt[:, AX], gt[:, AX], ACT.Exp, scale=-1.0))
                        me.do(A(gt[:, BETA], bac[:, :, 0:H], ACT.Exp, scale=-1.0))
                        me.do(A(ea[:, :], ea[:, :], ACT.Exp))
                        me.do(A(gt[:, AX], gt[:, AX], ACT.Ln, bias=C("ones")[:, 0:1]), "gates_act")
                    elif kind == "ss":
                        wait_filled(act, step)
                        if t >= 2:
                            act.wait_ge(S["qk_normed"], t - 1)
                        me.drain(A(rn[:, t % 2, :], small(step)[:, 0:CW], ACT.Ln, bias=C("eps")), step)
                        if t < 4:
                            me.do(A(rn[:, t % 2, :], rn[:, t % 2, :], ACT.Exp, bias=C("qscale"), scale=-0.5), "rn_done")
                        else:
                            me.do(A(rn[:, t % 2, :], rn[:, t % 2, :], ACT.Exp, scale=-0.5), "rn_done")
                    elif kind == "dcol":
                        wait_drained(act, step)
                        me.do(A(gt[:, ED], gt[:, ND], ACT.Exp, scale=-1.0), "ed_done")
                    elif kind == "D":
                        wait_filled(act, step)
                        if t:
                            if t == 2:
                                act.wait_ge(S["qs_done"], 1)
                            me.do(A(edl[:, t, :], wide(small(step))[:, :, L - 1], ACT.Exp))
                            me.do(A(eD[:, :, 0:L], wide(small(step)), ACT.Exp), "eD_done")
                        wait_drained(act, step)
                        me.do(A(lm[0:L, :, 0:L], lm[0:L, :, 0:L], ACT.Exp), "lm_done")
                    elif kind == "kt":
                        wait_filled(act, step)
                        for h in range(H):
                            ins = A(kt[0:L, h, :], small(step)[0:L, h * P:(h + 1) * P], ACT.Copy, scale=lm[0:L, h, L - 1:L])
                            me.drain(ins, step) if h == H - 1 else me.do(ins)
                    elif kind == "T1":
                        wait_filled(act, step)
                        me.drain(A(Vn[0:L, :, 0:L], wide(small(step))[0:L], ACT.Copy), step)
                    elif kind == "Y":
                        wait_filled(act, step)
                        me.drain(A(Ysb[0:L, :, 0:L], wide(small(step))[0:L], ACT.Copy), step)
                    elif kind == "vn":
                        wait_filled(act, step)
                        me.drain(A(vn[0:L, :, :].rearrange("p h v -> p (h v)"), small(step)[0:L, :], ACT.Copy), step)
                    elif kind == "o":
                        wait_filled(act, step)
                        me.do(A(qkv[:, 0:H, p0:p0 + L], wide(small(step)), ACT.Copy))
                        me.drain(A(osq[:, 0:H * L], small(step)[:, 0:H * L], ACT.Square), step)
                    elif kind in ("on", "cv"):
                        wait_filled(act, step)
                        i = NORMED.index(step)
                        if i:
                            act.wait_ge(S["gated"], i)
                        n, scale = (H * L, 1.0 / P) if kind == "on" else (T, 1.0)
                        rsqrt(rno[:, 0:n], small(step)[:, 0:n], scale, me, step, "gn_done")
                    elif kind == "btok":
                        wait_filled(act, step)
                        me.do(A(btk[0:L, t, :], small(step)[0:L, 0:256], ACT.Copy))
                        me.drain(A(btv[0:L, t, :], small(step)[0:L, 256:512], ACT.Copy), step)
                    elif kind == "bkc":
                        wait_filled(act, step)
                        me.drain(A(kcT[:, :, :].rearrange("p b t -> p (b t)"), small(step)[:, 0:256], ACT.Copy), step)
                    elif kind == "lc":
                        wait_filled(act, step)
                        me.drain(A(lastr[:, :], small(step)[0:2 * PAD * CB, 0:P], ACT.Copy), step)
                    elif kind == "sB":
                        act.wait_ge(S["maxima"], t + 1)
                        for n, (rows, a, b) in enumerate(((P, 0, P), (P, P, 3 * P), (DEC, 384, 576))):
                            me.do(A(prob[0:rows, a:b], prob[0:rows, a:b], ACT.Exp, bias=mx[0:rows, 0, n:n + 1],
                                    accum_out=mx[0:rows, 1, n:n + 1]), "exps" if n == 2 else None)
                    elif kind == "pT":
                        wait_filled(act, step)
                        me.do(A(pT[:, 0:448], small(step)[:, 0:448], ACT.Copy))
                        me.drain(A(pT[0:DEC, 448:512], small(step)[0:DEC, 448:512], ACT.Copy), step)
                    elif kind == "oB":
                        wait_filled(act, step)
                        r = slice(64 * (t % 2), 64 * (t % 2) + 64)
                        me.drain(A(tmp[r, 4 + t // 2, 0:T], small(step)[r, 0:T], ACT.Copy), step)
                    elif kind == "zs":
                        me.do(A(z[:, :, :], z[:, :, :], ACT.Silu), "z_done")
                        act.preload_act_table_set(LN_EXP)
                    elif kind == "gs":
                        me.do(A(gc[:, :, :], gc[:, :, :], ACT.Silu), "gc_done")
                        act.preload_act_table_set(LN_EXP)
                    elif kind == "oC":
                        wait_filled(act, step)
                        me.drain(A(oC[:, :, c0:c0 + L], small(step)[:, 0:256].rearrange("p (b l) -> p b l", b=2)[:, :, 0:L],
                                   ACT.Copy), step)
                    elif kind == "cm":
                        wait_drained(act, step)
                        act.wait_ge(S["qs_done"], 2)
                        me.do(A(tmp[:, 6 + t, 0:T], oC[:, t, :], ACT.Square), "oc_sq")
                    elif kind == "split":
                        k = SPLIT_ORDER[t]
                        if t == 0:
                            wait_products(layer, U_IN + 15)
                        elif t == 2:
                            act.wait_ge(S["gated"], len(NORMED))
                        me.do(A(hh[:, k, :], tmp[:, k, 0:T], ACT.Copy), "hh_done")

                for d in range(4):
                    split_hi(layer, U_OUT + d + 1)
                    act.wait_ge(S["x_updated"], SQ_OUT + d + 1)
                    at = slice(2 * d, 2 * d + 2)
                    me.do_at(A(tmp[:, at, 0:T], xT[:, at, :], ACT.Square), S["sq_done"], SQ_OUT + d + 1)
                statistics(1, me)
                apply_norm(3, 2, me)
                act.wait_ge(stored, (layer + 1) * 16 * STORES)
                ffn(layer, U_FFN2, 1, 3, me)
                statistics(2, me)

            for t, (_, _, L) in enumerate(TILES):
                for half in range(2):
                    act.wait_ge(S["y_turned"], 2 * t + half + 1)
                    me.do(A(tok[0:L, t, half * 512:half * 512 + 512], psum[0:L, 2 * t + half, :], ACT.Copy), "y_out")

        @block.vector
        def _(dve):
            V = dve

            def split_lo(layer, u, i=0, width=SLOT):
                dve.wait_ge(hi_done, layer * UNITS + 4 * i + u + 1)
                s = u % SPLIT
                V.tensor_tensor(wlo[:, s, 0:width], raw[:, u % RAW, 0:width], whi[:, s, 0:width].bitcast(F32),
                                ALU.subtract).then_inc(lo_done, 1)
                dve.wait_ge(lo_done, layer * UNITS + 4 * i + u + 1 + RAW)

            def wait_products(layer, u, i=0):
                dve.wait_ge(unit_used, layer * UNITS + 4 * i + u + 1 + SPLIT)

            def apply_norm(col, me):
                for k in range(KD):
                    me.do(V.scalar_tensor_tensor(tmp[:, k, 0:T], xT[:, k, :], par[:, col + k:col + k + 1], rstd[:, :],
                                                 ALU.mult, ALU.mult), "hf_done")

            def ffn(layer, u0, f, me):
                def gate_up(n, i):
                    u = u0 + 2 * n
                    at = bass.ds(2 * (2 * i + n), 2)
                    split_lo(layer, u + 1, i)
                    split_lo(layer, u + 2, i)
                    wait_products(layer, u + 1, i)
                    dve.wait_ge(S["gate_silu"], NJ * f + 2 * i + n + 1)
                    if n:
                        dve.wait_ge(S["act_hi_done"], NJ * f + 2 * i + n)
                    me.do_at(V.tensor_tensor(prod[:, :, :], gs[:, :, :], psum[:, 2:4, 0:T], ALU.mult), S["product"],
                              NJ * f + 2 * i + n + 1)
                    dve.wait_ge(S["act_hi_done"], NJ * f + 2 * i + n + 1)
                    me.do_at(V.tensor_tensor(act_lo[:, at, :], prod[:, :, :], act_hi[:, at, :].bitcast(F32),
                                              ALU.subtract), S["act_lo_done"], NJ * f + 2 * i + n + 1)

                def down(n, i):
                    u = u0 + 2 * NJ + 2 * n
                    for r in range(2):
                        if u + r + 1 < UNITS:
                            split_lo(layer, u + r + 1, i, SLOT if n == KD - 1 and r else DOWN_K * P)
                    wait_products(layer, u + 1, i)
                    x = xT[:, bass.ds(2 * i + n, 1), :].rearrange("p a t -> p (a t)")
                    me.do_at(V.scalar_tensor_tensor(x, psum[:, n % 2, 0:T], 0.5, x, ALU.mult, ALU.add), S["x_updated"],
                              SQ0[f] + 2 * i + n + 1)

                in_turn(dve, 1, NJ, 0, gate_up)
                in_turn(dve, 2, KD, 2, down)

            dve.drain().then_inc(arrived, 1)
            dve.wait_ge(par_turned, DEPTH)
            V.tensor_copy(par_all[:, :, :], psum[:, 5:5 + DEPTH, 0:NPAR]).then_inc(par_turned, 1)
            dve.wait_ge(par_turned, DEPTH + 1)
            with dve.Fori(0, DEPTH) as layer:
                split_lo(layer, 0)
                dve.wait_ge(layer_open, layer + 1)
                per_tile = lambda x: x[:, None, :].to_broadcast([P, 3, H])
                me = Engine(dve, "dve_step")
                me.do(V.tensor_copy(par[:, :], par_all[:, bass.ds(layer, 1), :].rearrange("p a n -> p (a n)")))
                apply_norm(R_F1, me)
                ffn(layer, U_FFN1, 0, me)
                dve.wait_ge(S["rstd_done"], 1)
                apply_norm(R_MIX, me)

                me.do(V.memset(up[:, :, 0:PAD], 0.0), "pads_zero")
                me.do(V.memset(bac[:, :, :], 0.0))
                me.do(V.memset(gt[:, ND], 0.0))
                me.do(V.memset(mx[:, :, :], 1.0))
                for step in STEPS:
                    kind, t = step[0], (step[1] if len(step) > 1 else None)
                    bank = small(step) if step in USE else None
                    if kind in PER_TILE:
                        c0, p0, L = TILES[t]
                        vb, kt, aT, Vt, U, Us, Vn, Ysb, lm = map(B[t].get, BUFFERS)
                        wide = lambda x: x[:, 0:H * L].rearrange("p (h l) -> p h l", h=H)
                        mask = lambda name: C(name, L, L)[:, None, :].to_broadcast([L, H, L])
                    if kind == "lo":
                        tail = t < len(IN_UNITS) and IN_UNITS[t][0] == "tail"
                        split_lo(layer, U_IN + t, 0, KD * P if tail else SLOT)
                    elif kind == "conv":
                        dve.wait_ge(S["unit_out"], CONV_UNIT[t] + 1)
                        for c in range(2):
                            b = 2 * t + c
                            for j in range(1, CONV_W):
                                me.do(V.scalar_tensor_tensor(qkv[:, b, :], up[:, 2 * (t % 2) + c, j:j + CW], tap(b, j),
                                                             qkv[:, b, :], ALU.mult, ALU.add),
                                      "conv_done" if c and j == CONV_W - 1 else None)
                    elif kind == "ba":
                        wait_filled(dve, step)
                        me.do(V.tensor_copy(bac[:, 0:2, :].rearrange("p t c -> p (t c)"), bank[:, 0:16]))
                        me.drain(V.tensor_copy(bac[0:DEC, 2, :], bank[0:DEC, 16:24]), step)
                        dve.wait_ge(gate_loaded, (layer + 1) * 32)
                        me.do(V.tensor_tensor(gt[:, GX], bac[:, :, H:2 * H], per_tile(dtb), ALU.add))
                        me.do(V.tensor_scalar(gt[:, RX], gt[:, GX], 0.0, None, ALU.max))
                        me.do(V.tensor_scalar(gt[:, AX], gt[:, GX], -1.0, None, ALU.mult))
                        me.do(V.tensor_tensor(gt[:, AX], gt[:, AX], gt[:, GX], ALU.max), "gates_in")
                    elif kind == "gates":
                        dve.wait_ge(S["gates_act"], 1)
                        me.do(V.tensor_tensor(gt[:, AX], gt[:, AX], gt[:, RX], ALU.add))
                        me.do(V.scalar_tensor_tensor(gt[:, G], gt[:, AX], -1.0, per_tile(ea), ALU.mult, ALU.mult))
                        me.do(V.tensor_scalar(gt[:, BETA], gt[:, BETA], 1.0, None, ALU.add))
                        me.do(V.reciprocal(gt[:, BETA], gt[:, BETA]), "gates_done")
                    elif kind == "ss":
                        dve.wait_ge(S["rn_done"], t + 1)
                        me.do(V.tensor_tensor(qkv[:, t, :], qkv[:, t, :], rn[:, t % 2, :], ALU.mult), "qk_normed")
                    elif kind == "dcol":
                        wait_filled(dve, step)
                        me.do(V.tensor_scalar(gt[:, ND, 0:2], bank[:, 0:8].rearrange("p (t h) -> p t h", h=H), -1.0, None,
                                              ALU.mult))
                        me.drain(V.tensor_scalar(gt[0:DEC, ND, 2], bank[0:DEC, 8:12], -1.0, None, ALU.mult), step)
                        dve.wait_ge(S["ed_done"], 1)
                        me.do(V.scalar_tensor_tensor(gt[:, NBE], gt[:, BETA], -1.0, gt[:, ED], ALU.mult, ALU.mult))
                    elif kind == "vt":
                        wait_filled(dve, step)
                        for h in range(H):
                            ins = V.tensor_scalar(vb[0:L, h, :], bank[0:L, h * P:(h + 1) * P], gt[0:L, BETA, t, h:h + 1],
                                                  None, ALU.mult)
                            me.drain(ins, step) if h == H - 1 else me.do(ins)
                    elif kind == "D":
                        if t:
                            dve.wait_ge(S["eD_done"], t)
                        if t == 2:
                            wait_drained(dve, ("kt", 1))
                        wait_filled(dve, step)
                        for h in range(H):
                            ins = V.scalar_tensor_tensor(lm[0:L, h, 0:L], bank[0:L, h * L:(h + 1) * L],
                                                         gt[0:L, ND, t, h:h + 1], C("future", L, L), ALU.add, ALU.add)
                            me.drain(ins, step) if h == H - 1 else me.do(ins)
                    elif kind == "G":
                        dve.wait_ge(S["lm_done"], t + 1)
                        wait_filled(dve, step)
                        me.drain(V.tensor_tensor(U[0:L, :, 0:L], wide(bank)[0:L], lm[0:L, :, 0:L], ALU.mult), step)
                        wait_filled(dve, ("Bb", t))
                        me.drain(V.tensor_tensor(U[0:L, :, 0:L], wide(small(("Bb", t)))[0:L], U[0:L, :, 0:L], ALU.mult),
                                 ("Bb", t))
                    elif kind == "QK":
                        wait_filled(dve, step)
                        me.drain(V.tensor_tensor(aT[0:L, :, 0:L], wide(bank)[0:L], lm[0:L, :, 0:L], ALU.mult), step)
                        if t:
                            q = qkv[:, 0:H, p0:p0 + L]
                            me.do(V.tensor_tensor(q, q, eD[:, :, 0:L], ALU.mult), "qs_done")
                        me.do(V.tensor_tensor(Vt[0:L, :, 0:L], U[0:L, :, 0:L], mask("level1"), ALU.mult))
                        me.do(V.tensor_tensor(Vt[0:L, :, 0:L], mask("ident"), Vt[0:L, :, 0:L], ALU.subtract))
                        me.do(V.tensor_tensor(Us[0:L, :, 0:L], U[0:L, :, 0:L], mask("level2"), ALU.mult), "tri_done")
                    elif kind == "Z":
                        s = step[2]
                        if s != LEVELS[t][-1]:
                            wait_filled(dve, ("Y", t, s))
                            me.do(V.tensor_tensor(Us[0:L, :, 0:L], U[0:L, :, 0:L], mask(f"level{2 * s}"), ALU.mult),
                                  "level_done")
                        wait_filled(dve, ("Zt", t, s))
                        if s != LEVELS[t][-1]:
                            wait_filled(dve, step)
                        me.drain(V.tensor_tensor(Vt[0:L, :, 0:L], Vt[0:L, :, 0:L], wide(small(("Zt", t, s)))[0:L],
                                                 ALU.subtract), ("Zt", t, s))
                        if s != LEVELS[t][-1]:
                            me.drain(V.tensor_tensor(Vn[0:L, :, 0:L], Vn[0:L, :, 0:L], wide(bank)[0:L], ALU.subtract), step)
                    elif kind == "kS":
                        wait_filled(dve, step)
                        for h in range(H):
                            ins = V.scalar_tensor_tensor(vb[0:L, h, :], bank[0:L, h * P:(h + 1) * P],
                                                         gt[0:L, NBE, t, h:h + 1], vb[0:L, h, :], ALU.mult, ALU.add)
                            me.drain(ins, step) if h == H - 1 else me.do(ins)
                    elif kind == "Su":
                        wait_filled(dve, step)
                        state = pS if t < 2 else sS
                        if t == 0:
                            me.drain(V.tensor_copy(state[:, :, :].rearrange("p h v -> p (h v)"), bank[:, :]), step)
                        else:
                            for h in range(H):
                                ins = V.scalar_tensor_tensor(state[:, h, :], state[:, h, :], edl[:, t, h:h + 1],
                                                             bank[:, h * P:(h + 1) * P], ALU.mult, ALU.add)
                                me.drain(ins, step) if h == H - 1 else me.do(ins)
                    elif kind == "on":
                        dve.wait_ge(S["gn_done"], NORMED.index(step) + 1)
                        dve.wait_ge(S["z_done"], 1)
                        dst = tmp[:, 0:H, c0:c0 + L]
                        me.do(V.tensor_tensor(dst, qkv[:, 0:H, p0:p0 + L], wide(rno), ALU.mult))
                        me.do(V.scalar_tensor_tensor(dst, dst, par[:, R_GDN:R_GDN + 1], z[:, :, c0:c0 + L], ALU.mult,
                                                     ALU.mult), "gated")
                    elif kind == "sA":
                        if t:
                            wait_filled(dve, ("pT", t - 1))
                        dve.wait_ge(S["bias_masked"], 1)
                        wait_filled(dve, step)
                        me.do(V.scalar_tensor_tensor(prob[:, 0:P], bank[:, 0:P], 0.125, bias[:, t, P:2 * P], ALU.mult,
                                                     ALU.add))
                        me.drain(V.scalar_tensor_tensor(prob[:, P:384], bank[:, P:384], 0.125, bias[:, t, :], ALU.mult,
                                                        ALU.add), step)
                    elif kind == "sB":
                        wait_filled(dve, step)
                        me.drain(V.scalar_tensor_tensor(prob[0:DEC, 384:576], bank[0:DEC, 0:192], 0.125,
                                                        bias[0:DEC, t, 0:192], ALU.mult, ALU.add), step)
                        parts = ((P, 0, P), (P, P, 384), (DEC, 384, 576))
                        for n, (rows, a, b) in enumerate(parts):
                            me.do(V.tensor_reduce(mx[0:rows, 0, n:n + 1], prob[0:rows, a:b], AX_X, ALU.max))
                        me.do(V.tensor_scalar(mx[:, 0, :], mx[:, 0, :], -1.0, None, ALU.mult), "maxima")
                        dve.wait_ge(S["exps"], t + 1)
                        me.do(V.reciprocal(mx[:, 2, :], mx[:, 1, :]))
                        for n, (rows, a, b) in enumerate(parts):
                            me.do(V.tensor_scalar(prob[0:rows, a:b], prob[0:rows, a:b], mx[0:rows, 2, n:n + 1], None,
                                                  ALU.mult), "probs" if n == 2 else None)
                    elif kind == "rot":
                        x = (bq, bk)[t // 2][:, t % 2, :]
                        wait_filled(dve, step)
                        me.drain(V.tensor_tensor(rsc[:, :], bank[:, 0:T], C("sin"), ALU.mult), step)
                        me.do(V.tensor_tensor(x, x, C("cos"), ALU.mult))
                        me.do(V.tensor_tensor(x, x, rsc[:, :], ALU.add), "rope_done")
                    elif kind == "ctok":
                        wait_filled(dve, step)
                        gk = C(f"gk{L}", L)[:, :, None].to_broadcast([L, H, 64])
                        me.do(V.tensor_tensor(ctk[0:L, :].rearrange("p (h d) -> p h d", h=H),
                                              bank[0:L, 0:256].rearrange("p (h d) -> p h d", h=H), gk, ALU.mult))
                        me.drain(V.tensor_copy(ctv[0:L, :], bank[0:L, 256:512]), step)
                    elif kind == "cqk":
                        wait_filled(dve, step)
                        at, _ = CAT["dmask0"]
                        decay = cst[:, at:at + H * P].rearrange("p (h l) -> p h l", h=H)
                        if L < P:
                            me.do(V.memset(aC[L:P, :, 0:L], 0.0))
                        me.drain(V.tensor_tensor(aC[0:L, :, 0:L], wide(bank)[0:L], decay[0:L, :, 0:L], ALU.mult), step)
                        if t:
                            at, _ = CAT["gq0"]
                            gq = cst[:, at:at + 2 * P].rearrange("p (b l) -> p b l", b=2)
                            me.do(V.tensor_tensor(bq[:, :, c0:c0 + L], bq[:, :, c0:c0 + L], gq[:, :, 0:L], ALU.mult),
                                  "qd_done")
                    elif kind == "R":
                        wait_filled(dve, step)
                        rstate = pR if t < 2 else sR
                        if t == 0:
                            me.drain(V.tensor_copy(rstate[:, :, :].rearrange("p b v -> p (b v)"), bank[:, 0:P]), step)
                        else:
                            for b in range(2):
                                ins = V.scalar_tensor_tensor(rstate[:, b, :], rstate[:, b, :], C(f"gl{L}")[:, b:b + 1],
                                                             bank[:, b * 64:b * 64 + 64], ALU.mult, ALU.add)
                                me.drain(ins, step) if b else me.do(ins)
                    elif kind == "cm":
                        wait_filled(dve, step)
                        me.drain(V.tensor_tensor(oC[:, t, :], oC[:, t, :], bank[:, 0:T], ALU.subtract), step)
                    elif kind == "cv":
                        dve.wait_ge(S["gn_done"], NORMED.index(step) + 1)
                        dve.wait_ge(S["gc_done"], 1)
                        dst = tmp[:, 6 + t, 0:T]
                        me.do(V.tensor_tensor(dst, oC[:, t, :], rno[:, 0:T], ALU.mult))
                        me.do(V.tensor_tensor(dst, dst, gc[:, t, :], ALU.mult), "gated")

                for d in range(4):
                    split_lo(layer, U_OUT + d + 1)
                    wait_products(layer, U_OUT + d)
                    x = xT[:, 2 * d:2 * d + 2, :]
                    me.do_at(V.tensor_tensor(x, psum[:, 2 * (d % 2):2 * (d % 2) + 2, 0:T], x, ALU.add), S["x_updated"],
                              SQ_OUT + d + 1)
                dve.wait_ge(S["rstd_done"], 2)
                apply_norm(R_F2, me)
                ffn(layer, U_FFN2, 1, me)
                dve.drain().then_inc(arrived, 1)

            dve.wait_ge(S["rstd_done"], 3)
            for k in range(KD):
                me.do(V.scalar_tensor_tensor(tmp[:, k, 0:T], xT[:, k, :], par[:, R_FINAL + k:R_FINAL + k + 1],
                                             rstd[:, :], ALU.mult, ALU.mult), "y_normed")


_INS = ["x_prompt", "x_sample", "state_gdn", "state_conv", "cache_band_k", "cache_band_v", "state_ret", "norm_ffn1",
        "w_ffn1_gate", "w_ffn1_up", "w_ffn1_down", "norm_mix", "w_in", "conv_w", "a_log", "dt_bias", "gdn_norm",
        "rel_bias", "w_out", "norm_ffn2", "w_ffn2_gate", "w_ffn2_up", "w_ffn2_down", "norm_final"]
_OUTS = [(1, SEQ, D_MODEL), (1, DEC, D_MODEL),
         (DEPTH, 1, H, 128, 128), (DEPTH, 1, PAD, CONV_DIM), (DEPTH, 1, SEQ, H, 64), (DEPTH, 1, SEQ, H, 64),
         (DEPTH, 1, H, 64, 64),
         (DEPTH, 1, H, 128, 128), (DEPTH, 1, PAD, CONV_DIM), (DEPTH, 1, DEC, H, 64), (DEPTH, 1, DEC, H, 64),
         (DEPTH, 1, H, 64, 64)]


def kernel(**inputs):
    import concourse.bacc as bacc
    from concourse.bass_utils import run_bass_kernel_spmd

    nc = bacc.Bacc("TRN2", target_bir_lowering=False, num_devices=1)
    arrays, args = {}, []
    for name in _INS:
        arrays[f"in_{name}"] = np.ascontiguousarray(inputs[name])
    arrays["in_consts"] = constants()[0]
    for name, a in arrays.items():
        args.append(nc.dram_tensor(name, a.shape, mybir.dt.from_np(a.dtype), kind="ExternalInput").ap())
    for i, shape in enumerate(_OUTS):
        args.append(nc.dram_tensor(f"out_{i}", shape, F32, kind="ExternalOutput").ap())
    build(nc, *args)
    r = run_bass_kernel_spmd(nc, [arrays], core_ids=[0])
    return tuple(r.results[0][f"out_{i}"] for i in range(len(_OUTS)))
```
